# Optimizing a Trainium2 kernel written in Bass

```python
import math
import jax, jax.numpy as jnp
from jax import lax
import numpy as np

D_MODEL = 1024
BATCH = 1
SEQ = 512
DEPTH = 1

N_HEADS = 8
QK_NOPE_DIM = 64
QK_ROPE_DIM = 32
QK_DIM = QK_NOPE_DIM + QK_ROPE_DIM
V_HEAD_DIM = 64
Q_LORA_RANK = 256
KV_LORA_RANK = 128
ROPE_THETA = 10000.0
Q_BLOCK = 128
ATTN_WIDTH = N_HEADS * V_HEAD_DIM

LRU_WIDTH = 512
LRU_BLOCKS = 4
LRU_BLOCK_DIM = LRU_WIDTH // LRU_BLOCKS
CONV_WIDTH = 4
CONV_LEFT = 2
LRU_C = 8.0
N_DIRS = 2

N_BRANCHES = 2
D_FF = -(-8 * D_MODEL // (3 * 256)) * 256
NORM_EPS = 1e-6

C_QA = Q_LORA_RANK
C_KVA = C_QA + KV_LORA_RANK
C_KR = C_KVA + QK_ROPE_DIM
C_LX = C_KR + LRU_WIDTH
C_LY = C_LX + LRU_WIDTH
D_IN = C_LY + N_BRANCHES * D_MODEL

kernel_name = 'hybrid_mla_rglru_encoder'

def rmsnorm(x, g):
    xf = x.astype(jnp.float32)
    y = xf * lax.rsqrt(jnp.mean(xf * xf, axis=-1, keepdims=True) + NORM_EPS)
    return (y * g.astype(jnp.float32)).astype(x.dtype)

def rope_tables(seq):
    pos = jnp.arange(seq, dtype=jnp.float32)
    inv_freq = 1.0 / (ROPE_THETA ** (jnp.arange(0, QK_ROPE_DIM, 2, dtype=jnp.float32) / QK_ROPE_DIM))
    ang = pos[:, None] * inv_freq[None, :]
    return jnp.cos(ang), jnp.sin(ang)

def apply_rope(x, cos, sin):
    x1, x2 = jnp.split(x, 2, axis=-1)
    cos = cos.astype(x.dtype)
    sin = sin.astype(x.dtype)
    return jnp.concatenate([x1 * cos - x2 * sin, x2 * cos + x1 * sin], axis=-1)

def mla_mixer(q_a, kv_a, k_rope_raw, q_a_norm_g, w_q_b, kv_a_norm_g, w_kv_b):
    b, s, _ = q_a.shape
    cos, sin = rope_tables(s)
    q = (rmsnorm(q_a, q_a_norm_g) @ w_q_b).reshape(b, s, N_HEADS, QK_DIM)
    q_nope, q_rope = q[..., :QK_NOPE_DIM], q[..., QK_NOPE_DIM:]
    q_rope = apply_rope(q_rope, cos[:, None, :], sin[:, None, :])
    kv = (rmsnorm(kv_a, kv_a_norm_g) @ w_kv_b).reshape(b, s, N_HEADS, QK_NOPE_DIM + V_HEAD_DIM)
    k_nope, v = kv[..., :QK_NOPE_DIM], kv[..., QK_NOPE_DIM:]
    k_rope = apply_rope(k_rope_raw, cos, sin)
    q = jnp.concatenate([q_nope, q_rope], axis=-1)
    k = jnp.concatenate([k_nope, jnp.broadcast_to(k_rope[:, :, None, :], (b, s, N_HEADS, QK_ROPE_DIM))], axis=-1)
    scale = QK_DIM ** -0.5
    n_blk = s // Q_BLOCK
    q_blocks = q.reshape(b, n_blk, Q_BLOCK, N_HEADS, QK_DIM).transpose(1, 0, 2, 3, 4)

    def attend(qb):
        sc = jnp.einsum('bqhd,bkhd->bhqk', qb, k).astype(jnp.float32) * scale
        p = jax.nn.softmax(sc, axis=-1).astype(v.dtype)
        return jnp.einsum('bhqk,bkhd->bqhd', p, v)

    o = lax.map(attend, q_blocks)
    return o.transpose(1, 0, 2, 3, 4).reshape(b, s, ATTN_WIDTH)

def _lin_combine(left, right):
    a1, b1 = left
    a2, b2 = right
    return a1 * a2, a2 * b1 + b2

def rglru_bidir(xl, conv_w, conv_b, w_r, b_r, w_i, b_i, lam):
    b, s, w = xl.shape
    xp = jnp.pad(xl, ((0, 0), (CONV_LEFT, CONV_WIDTH - 1 - CONV_LEFT), (0, 0)))
    xc = sum(xp[:, j:j + s, :] * conv_w[j] for j in range(CONV_WIDTH)) + conv_b
    xb = xc.reshape(b, s, LRU_BLOCKS, LRU_BLOCK_DIM)
    r = jax.nn.sigmoid((jnp.einsum('bsnc,rncd->rbsnd', xb, w_r) + b_r[:, None, None]).astype(jnp.float32))
    i = jax.nn.sigmoid((jnp.einsum('bsnc,rncd->rbsnd', xb, w_i) + b_i[:, None, None]).astype(jnp.float32))
    r = r.reshape(N_DIRS, b, s, w)
    i = i.reshape(N_DIRS, b, s, w)
    log_a = -LRU_C * r * jax.nn.softplus(-lam.astype(jnp.float32))[:, None, None, :]
    a = jnp.exp(log_a)
    mult = jnp.sqrt(-jnp.expm1(2.0 * log_a))
    u = i * xc.astype(jnp.float32)[None] * mult
    _, h_fwd = lax.associative_scan(_lin_combine, (a[0], u[0]), axis=1)
    _, h_bwd = lax.associative_scan(_lin_combine, (a[1], u[1]), axis=1, reverse=True)
    return (h_fwd + h_bwd).astype(xl.dtype)

def setup_inputs(seed: int = 0) -> dict:
    key = jax.random.key(seed)
    ks = jax.random.split(key, 24)
    f32 = jnp.float32
    L = DEPTH

    def nrm(k, shape, fan_in):
        return jax.random.normal(k, shape, f32) * (fan_in ** -0.5)

    def gain(k, shape):
        return jnp.ones(shape, f32) + 0.01 * jax.random.normal(k, shape, f32)

    u = jax.random.uniform(ks[14], (L, N_DIRS, LRU_WIDTH), f32, 0.9, 0.999)
    a0 = u ** (1.0 / LRU_C)
    lru_lambda = jnp.log(a0) - jnp.log1p(-a0)
    return {
        'x': jax.random.normal(ks[0], (BATCH, SEQ, D_MODEL), f32),
        'norm1_g': gain(ks[1], (L, D_MODEL)),
        'w_in': nrm(ks[2], (L, D_MODEL, D_IN), D_MODEL),
        'q_a_norm_g': gain(ks[3], (L, Q_LORA_RANK)),
        'w_q_b': nrm(ks[4], (L, Q_LORA_RANK, N_HEADS * QK_DIM), Q_LORA_RANK),
        'kv_a_norm_g': gain(ks[5], (L, KV_LORA_RANK)),
        'w_kv_b': nrm(ks[6], (L, KV_LORA_RANK, N_HEADS * (QK_NOPE_DIM + V_HEAD_DIM)), KV_LORA_RANK),
        'w_o_attn': nrm(ks[7], (L, ATTN_WIDTH, D_MODEL), ATTN_WIDTH),
        'conv_w': nrm(ks[8], (L, CONV_WIDTH, LRU_WIDTH), CONV_WIDTH),
        'conv_b': 0.1 * jax.random.normal(ks[9], (L, LRU_WIDTH), f32),
        'w_rgate': nrm(ks[10], (L, N_DIRS, LRU_BLOCKS, LRU_BLOCK_DIM, LRU_BLOCK_DIM), LRU_BLOCK_DIM),
        'b_rgate': 0.1 * jax.random.normal(ks[11], (L, N_DIRS, LRU_BLOCKS, LRU_BLOCK_DIM), f32),
        'w_igate': nrm(ks[12], (L, N_DIRS, LRU_BLOCKS, LRU_BLOCK_DIM, LRU_BLOCK_DIM), LRU_BLOCK_DIM),
        'b_igate': 0.1 * jax.random.normal(ks[13], (L, N_DIRS, LRU_BLOCKS, LRU_BLOCK_DIM), f32),
        'lru_lambda': lru_lambda,
        'w_o_lru': nrm(ks[15], (L, LRU_WIDTH, D_MODEL), LRU_WIDTH),
        'w_out': nrm(ks[16], (L, D_MODEL, D_MODEL), D_MODEL),
        'norm2_g': gain(ks[17], (L, D_MODEL)),
        'w_ffn_gate': nrm(ks[18], (L, D_MODEL, D_FF), D_MODEL),
        'w_ffn_up': nrm(ks[19], (L, D_MODEL, D_FF), D_MODEL),
        'w_ffn_down': nrm(ks[20], (L, D_FF, D_MODEL), D_FF),
        'final_g': gain(ks[21], (D_MODEL,)),
    }

def reference(x, norm1_g, w_in, q_a_norm_g, w_q_b, kv_a_norm_g, w_kv_b, w_o_attn,
              conv_w, conv_b, w_rgate, b_rgate, w_igate, b_igate, lru_lambda, w_o_lru,
              w_out, norm2_g, w_ffn_gate, w_ffn_up, w_ffn_down, final_g):
    for l in range(DEPTH):
        h = rmsnorm(x, norm1_g[l])
        proj = h @ w_in[l]
        q_a = proj[..., :C_QA]
        kv_a = proj[..., C_QA:C_KVA]
        k_rope_raw = proj[..., C_KVA:C_KR]
        lru_x = proj[..., C_KR:C_LX]
        lru_y = proj[..., C_LX:C_LY]
        gate_logits = proj[..., C_LY:]

        attn = mla_mixer(q_a, kv_a, k_rope_raw, q_a_norm_g[l], w_q_b[l], kv_a_norm_g[l], w_kv_b[l]) @ w_o_attn[l]
        rec = rglru_bidir(lru_x, conv_w[l], conv_b[l], w_rgate[l], b_rgate[l], w_igate[l], b_igate[l], lru_lambda[l])
        rec = (jax.nn.gelu(lru_y) * rec) @ w_o_lru[l]

        gates = jax.nn.sigmoid(gate_logits.astype(jnp.float32)).astype(x.dtype)
        g_attn = gates[..., :D_MODEL]
        g_rec = gates[..., D_MODEL:]
        merged = g_attn * attn + g_rec * rec
        x = x + merged @ w_out[l]

        h2 = rmsnorm(x, norm2_g[l])
        x = x + (jax.nn.silu(h2 @ w_ffn_gate[l]) * (h2 @ w_ffn_up[l])) @ w_ffn_down[l]
    return rmsnorm(x, final_g)


_drawn_inputs = setup_inputs


def setup_inputs(seed=0):
    import zlib

    import numpy as np

    out = dict(_drawn_inputs(seed))
    spreads = {}
    factors = {'norm1_g': 8.0,
     'q_a_norm_g': 30.83,
     'kv_a_norm_g': 27.721,
     'b_rgate': 7.751,
     'b_igate': 3.865,
     'norm2_g': 39.557,
     'final_g': 30.215}
    for name, (base, spread) in spreads.items():
        noise = np.random.default_rng([zlib.crc32(name.encode()), seed]).standard_normal(out[name].shape)
        drawn = base * np.exp(spread * noise) if base else spread * noise
        out[name] = __import__('jax').numpy.asarray(drawn.astype(out[name].dtype))
    for name, factor in factors.items():
        out[name] = (out[name] * factor).astype(out[name].dtype)
    return out
```

```python
from contextlib import ExitStack

import numpy as np

import concourse.bass as bass
from concourse import mybir

P = 128
ALU = mybir.AluOpType
ACT = mybir.ActivationFunctionType
AX_X = mybir.AxisListType.X
F32 = mybir.dt.float32
F32R = mybir.dt.float32r

D = 1024
SEQ = 512
KD = D // P
NT = SEQ // P
HEADS, NOPE, ROPE, VD = 8, 64, 32, 64
QK = NOPE + ROPE
HALF = ROPE // 2
QL, KVL = 256, 128
CA = QL + KVL + ROPE
W = 512
NB = W // P
TAPS, LEFT = 4, 2
LRU_C = 8.0
FF = 2816
FT = FF // P
EPS = 1e-6
SCALE = float(QK) ** -0.5
C_LX, C_LY, C_G = CA, CA + W, CA + 2 * W

T_X, T_A, T_G0, T_Y, T_G1, T_V = 0, 4, 8, 10, 14, 15
T_HEAD = 16
T_R = T_HEAD + 4 * HEADS
T_OUT = T_R + 8
T_FFN = T_OUT + 8
T_DN = T_FFN + 2 * FT
PAIR_INC = 48

ROW_G1, ROW_G2, ROW_GQ, ROW_GKV, ROW_CW, ROW_CB, ROW_BR, ROW_BI, ROW_LAM = 0, 8, 16, 18, 19, 35, 39, 47, 55
N_ROWS = 63


def rope_constants():
    inv = (1.0 / (np.float32(10000.0) ** (np.arange(0, ROPE, 2, dtype=np.float32) / np.float32(ROPE)))).astype(np.float32)
    ang = np.arange(SEQ, dtype=np.float32)[:, None] * inv[None, :]
    cos, sin = np.cos(ang).astype(np.float32), np.sin(ang).astype(np.float32)
    q = np.concatenate([np.ones((NOPE, SEQ), np.float32), cos.T, cos.T, -sin.T, sin.T], axis=0)
    k = np.stack([cos, sin], axis=1).reshape(NT, P, 2, HALF).transpose(1, 0, 2, 3)
    return np.ascontiguousarray(q), np.ascontiguousarray(k)


def build(nc, x, norm1_g, w_in, q_a_norm_g, w_q_b, kv_a_norm_g, w_kv_b, w_o_attn, conv_w, conv_b,
          w_rgate, b_rgate, w_igate, b_igate, lru_lambda, w_o_lru, w_out, norm2_g, w_ffn_gate,
          w_ffn_up, w_ffn_down, final_g, rope_q, rope_k, out):
    x_v = x[0].rearrange("(t p) n -> p t n", p=P)
    out_v = out[0].rearrange("(t p) n -> p t n", p=P)
    w_in_v = w_in[0].rearrange("(k p) n -> p k n", p=P)
    w_qb_v = w_q_b[0].rearrange("(k p) n -> p k n", p=P)
    w_kvb_v = w_kv_b[0]
    w_val_v = w_kv_b[0].rearrange("p (h a c) -> p h a c", a=2, c=VD)
    w_r_v = w_rgate[0].rearrange("r n c d -> c r n d")
    w_i_v = w_igate[0].rearrange("r n c d -> c r n d")
    w_ol_v = w_o_lru[0].rearrange("(k p) n -> p k n", p=P)
    w_oa_v = w_o_attn[0].rearrange("(k p) n -> p k n", p=P)
    w_out_v = w_out[0].rearrange("(k p) n -> p k n", p=P)
    w_fg_v = w_ffn_gate[0].rearrange("(k p) n -> p k n", p=P)
    w_fu_v = w_ffn_up[0].rearrange("(k p) n -> p k n", p=P)
    w_fd_v = w_ffn_down[0].rearrange("(k p) n -> p k n", p=P)

    with ExitStack() as ctx:
        def sb(name, shape, dt=F32):
            return ctx.enter_context(nc.sbuf_tensor(name, shape, dt))

        def sem(name):
            return ctx.enter_context(nc.semaphore(name))

        ident = sb("ident", [P, P])
        rows = sb("rows", [64, P])
        prm = sb("prm", [P, 64])
        xt = sb("xt", [P, NT, D])
        hT_hi = sb("hT_hi", [P, KD, SEQ], F32R)
        hT_lo = sb("hT_lo", [P, KD, SEQ], F32R)
        raw = sb("raw", [P, 2, 2048])
        w_hi = sb("w_hi", [P, 4, 1024], F32R)
        w_lo = sb("w_lo", [P, 4, 1024], F32R)
        store = sb("store", [P, FT, SEQ])
        lru_h = sb("lru_h", [P, NB, SEQ])
        lru_y = sb("lru_y", [P, NB, SEQ])
        val = sb("val", [P, NT, HEADS * VD])
        prob = sb("prob", [P, NT, SEQ])
        f_hi = sb("f_hi", [P, 8, SEQ], F32R)
        f_lo = sb("f_lo", [P, 8, SEQ], F32R)
        tab_q = sb("tab_q", [P, SEQ])
        tab_k = sb("tab_k", [P, NT, 2, HALF])
        fin_g = sb("fin_g", [P, D])
        ksc = sb("ksc", [P, 4, NT, HALF])
        o_half = sb("o_half", [P, SEQ])
        ssq = sb("ssq", [P, 4, 8])
        rms = sb("rms", [P, 4, 8])
        rstd = sb("rstd", [P, 4, 8])
        sp = sb("sp", [P, 8, 8])
        decay = sb("decay", [P, 3, 8])
        mx = sb("mx", [P, NT])
        nbias = sb("nbias", [P, NT])
        psum_p = sb("psum_p", [P, NT])
        rsum = sb("rsum", [P, NT])
        ps = ctx.enter_context(nc.psum_tensor("ps", [P, 8, SEQ], F32))

        FQA, FKVA, FK, FQ, FPT, FV = 0, 2, 3, 4, 5, 7
        FXC, FREC, FO, FACT = 4, 4, 0, 0

        xp = store[:, 0:5, :].rearrange("p a n -> p (a n)")[:, 0:NB * (SEQ + TAPS - 1)].rearrange(
            "p (n s) -> p n s", n=NB)
        pa = store[:, 5:9, 0:CA]
        lru_a = store[:, 8:12, :]
        lru_t = store[:, 12:16, :]
        xc = store[:, 16:20, :]
        o_t = store[:, 16:20, :]
        q_f, q_s = store[:, 20, :], store[:, 21, :]
        lru_r = xt[:, 0:2, :].rearrange("p t (a n) -> p (t a) n", a=2)
        lru_i = xt[:, 2:4, :].rearrange("p t (a n) -> p (t a) n", a=2)
        xn = store[:, 0:8, :].rearrange("p (t a) n -> p t (a n)", a=2)
        sq_junk = prob[:, :, :].rearrange("p (t a) n -> p t (a n)", a=2)
        silu = prob[:, 0:2, :]

        x_in = [sem(f"x_in{t}") for t in range(NT)]
        x_back = sem("x_back")
        prm_in, tab_in, fin_in = sem("prm_in"), sem("tab_in"), sem("fin_in")
        raw_in = [sem("raw_in0"), sem("raw_in1")]
        w_half = sem("w_half")
        w_ready = sem("w_ready")
        w_used = sem("w_used")
        s_ident, s_pad = sem("ident_ready"), sem("pad_ready")
        prm_t, prm_ready = sem("prm_t"), sem("prm_ready")
        ssq_ready, rms_ready, rstd_ready = sem("ssq_ready"), sem("rms_ready"), sem("rstd_ready")
        xn_ready, xT_done, h_half, h_ready = sem("xn_ready"), sem("xT_done"), sem("h_half"), sem("h_ready")
        xp_ready, xc_full, xc_half, xc_ready = (
            sem("xp_ready"), sem("xc_full"), sem("xc_half"), sem("xc_ready"))
        a_done, pa_ready, pa_norm, aT_done, aT_half, aT_ready = (
            sem("a_done"), sem("pa_ready"), sem("pa_norm"), sem("aT_done"), sem("aT_half"), sem("aT_ready"))
        lam_neg, lam_exp, decay_ready = sem("lam_neg"), sem("lam_exp"), sem("decay_ready")
        g_done, sig_ready, exp3_ready, m2_ready, mult_ready, scan_done = (
            sem("g_done"), sem("sig_ready"), sem("exp3_ready"), sem("m2_ready"), sem("mult_ready"), sem("scan_done"))
        y_ready, rec_full, rec_half, rec_ready = (
            sem("y_ready"), sem("rec_full"), sem("rec_half"), sem("rec_ready"))
        v_done, v_ready = sem("v_done"), sem("v_ready")
        q_prod, q_full, q_half, q_ready, k_half, k_ready = (
            sem("q_prod"), sem("q_full"), sem("q_half"), sem("q_ready"),
            sem("k_half"), sem("k_ready"))
        vs_half, vs_ready = sem("vs_half"), sem("vs_ready")
        sc_done, max_ready, nb_ready, e_ready, rs_ready, p_ready = (
            sem("sc_done"), sem("max_ready"), sem("nb_ready"), sem("e_ready"), sem("rs_ready"), sem("p_ready"))
        gl_ready = sem("gl_ready")
        t_done, pt_half, pt_ready, pv_done = sem("t_done"), sem("pt_half"), sem("pt_ready"), sem("pv_done")
        oc_ready, o_ready, ot_half, ot_ready = sem("oc_ready"), sem("o_ready"), sem("ot_half"), sem("ot_ready")
        gs_ready = sem("gs_ready")
        rl_done, ra_done, rl_gated, ra_gated, mg_full, mg_half, mg_ready = (
            sem("rl_done"), sem("ra_done"), sem("rl_gated"), sem("ra_gated"), sem("mg_full"), sem("mg_half"),
            sem("mg_ready"))
        wo_done, x2_ready, h2_half, h2_ready = sem("wo_done"), sem("x2_ready"), sem("h2_half"), sem("h2_ready")
        silu_ready, act_ready = sem("silu_ready"), sem("act_ready")
        act_half, act_split = sem("act_half"), sem("act_split")
        dn_done, y2_ready, fin_ready, stored = sem("dn_done"), sem("y2_ready"), sem("fin_ready"), sem("stored")
        dve_step = sem("dve_step")
        block = ctx.enter_context(nc.Block())

        def raw_view(kind, slot, j):
            r = raw[:, slot, :]
            if kind == "cols":
                return r.rearrange("p (k n) -> p k n", k=KD)[:, :, P * j:P * j + P]
            if kind == "a":
                return r[:, 0:4 * CA].rearrange("p (k n) -> p k n", k=4)[:, 2 * j:2 * j + 2, :]
            if kind == "wo":
                return r.rearrange("p (k n) -> p k n", k=4)[:, :, 256 * j:256 * j + 256]
            if kind == "k":
                return r[:, 1024:1024 + P]
            if kind == "v":
                return r[:, 1024:1024 + 512]
            return r[:, 1024 * j:1024 * j + 1024]

        def split_view(w, kind, slot):
            s = w[:, slot, :]
            if kind == "cols":
                return s.rearrange("p (k n) -> p k n", k=KD)
            if kind == "a":
                return s[:, 0:2 * CA].rearrange("p (k n) -> p k n", k=2)
            if kind == "wo":
                return s.rearrange("p (k n) -> p k n", k=4)
            if kind == "k":
                return s[:, 0:P]
            if kind == "v":
                return s[:, 0:512]
            return s

        def q_views(w, slot):
            src = raw[:, 0, 0:2 * QK].rearrange("p (k n) -> p k n", k=2)
            dst = w[:, slot, 0:2 * P].rearrange("p (k n) -> p k n", k=2)
            halves = src[:, :, NOPE:QK].rearrange("p k (b n) -> p k b n", b=2)
            return [(dst[:, :, 0:QK], src),
                    (dst[:, :, QK:QK + HALF], halves[:, :, 1, :]),
                    (dst[:, :, QK + HALF:P], halves[:, :, 0, :])]

        def kind_of(t):
            if t < T_A or T_Y <= t < T_G1:
                return "cols"
            if t < T_G0:
                return "a"
            if t == T_V:
                return "v"
            if t < T_HEAD:
                return "plain"
            if t < T_R:
                return ("q", "k", "cols", "cols")[(t - T_HEAD) % 4]
            if t < T_OUT:
                return "wo"
            if t < T_FFN:
                return "plain"
            return "cols" if t < T_DN else "plain"

        def tiles_in(t):
            return 2 if t == T_G0 else 1

        def split_hi(act, t0, dt=0):
            kind = kind_of(t0)
            if t0 % 2 == 0:
                act.wait_ge(raw_in[t0 // 2 % 2], dt * (PAIR_INC // 4) + PAIR_INC * (t0 // 4 + 1))
            if t0 >= 4:
                act.wait_ge(w_used, dt + t0 - 3)
            if kind == "q":
                for dst, src in q_views(w_hi, t0 % 4):
                    last = nc.scalar.activation(dst, src, ACT.Copy)
            else:
                last = nc.scalar.activation(split_view(w_hi, kind, t0 % 4), raw_view(kind, t0 // 2 % 2, t0 % 2), ACT.Copy)
            last.then_inc(w_half, tiles_in(t0))

        def split_lo(dve, t0, dt=0):
            kind = kind_of(t0)
            dve.wait_ge(w_half, dt + t0 + tiles_in(t0))
            if kind == "q":
                for (dst, src), (hi, _) in zip(q_views(w_lo, t0 % 4), q_views(w_hi, t0 % 4)):
                    last = nc.vector.tensor_tensor(dst, src, hi.bitcast(F32), ALU.subtract)
            else:
                last = nc.vector.tensor_tensor(split_view(w_lo, kind, t0 % 4), raw_view(kind, t0 // 2 % 2, t0 % 2),
                                               split_view(w_hi, kind, t0 % 4).bitcast(F32), ALU.subtract)
            last.then_inc(w_ready, tiles_in(t0))

        def tile_used(eng, t):
            eng.wait_ge(w_used, t + 1)

        def a_done_wait(eng, t):
            if t < NT - 1:
                eng.wait_ge(a_done, t + 1)
            else:
                tile_used(eng, T_A + 3)

        def gates_done(eng, d, part, n):
            if part and n == NB - 1:
                eng.wait_ge(w_used, T_G1 + 1 if d else T_G0 + 2)
            else:
                eng.wait_ge(g_done, (2 * NB - 1) * d + NB * part + n + 1)

        def v_done_wait(eng, t):
            if t < NT - 1:
                eng.wait_ge(v_done, t + 1)
            else:
                tile_used(eng, T_V)

        def branch_done(eng, first, branch, m):
            if m % 2 == 0:
                eng.wait_ge(first, m // 2 + 1)
            else:
                tile_used(eng, T_R + 4 * (m // 4) + 2 * branch + m % 4 // 2)

        def w_out_done(eng, c, t):
            if t < NT - 1:
                eng.wait_ge(wo_done, (NT - 1) * c + t + 1)
            else:
                tile_used(eng, T_OUT + 4 * c + 3)

        def product(dst, l_hi, l_lo, r_hi, r_lo, start, stop):
            nc.tensor.matmul(dst, l_lo, r_hi, start=start, stop=False)
            nc.tensor.matmul(dst, l_hi, r_lo, start=False, stop=False)
            return nc.tensor.matmul(dst, l_hi, r_hi, start=False, stop=stop)

        @block.sync
        def _(sync):
            def load(p0, dp, dst, src, inc=PAIR_INC):
                if p0 >= 2:
                    sync.wait_ge(w_ready, dp * 2 + 2 * p0 - 2)
                sync.dma_start(dst, src).then_inc(raw_in[p0 % 2], inc)

            def slot(p0):
                return raw[:, p0 % 2, :]

            def k_major(p0, k):
                return slot(p0).rearrange("p (k n) -> p k n", k=k)

            for t in range(NT):
                sync.dma_start(xt[:, t, :], x_v[:, t, :]).then_inc(x_in[t], 16)
            for p in (0, 1):
                load(p, 0, k_major(p, KD), w_in_v[:, :, C_LX + 256 * p:C_LX + 256 * p + 256])
            for p in (2, 3):
                load(p, 0, slot(p)[:, 0:4 * CA].rearrange("p (k n) -> p k n", k=4),
                     w_in_v[:, 4 * (p - 2):4 * (p - 2) + 4, 0:CA])

            def load_lru_gates(p, d, inc):
                for part, src in ((0, w_r_v), (1, w_i_v)):
                    load(p, 0, slot(p)[:, 512 * part:512 * part + 512].rearrange("p (n d) -> p n d", n=NB),
                         src[:, d, :, :], inc=inc if part else 16)
            load_lru_gates(4, 0, 32)
            for p in (5, 6):
                load(p, 0, k_major(p, KD), w_in_v[:, :, C_LY + 256 * (p - 5):C_LY + 256 * (p - 5) + 256])
            load_lru_gates(7, 1, 16)
            load(7, 0, slot(7)[:, 1024:1536].rearrange("p (h c) -> p h c", h=HEADS), w_val_v[:, :, 1, :], inc=16)
            p_head = T_HEAD // 2
            with sync.Fori(0, HEADS) as h:
                load(p_head, h * 2, slot(p_head)[:, 0:2 * QK].rearrange("p (k n) -> p k n", k=2),
                     w_qb_v[:, :, bass.ds(h * QK, QK)], inc=32)
                sync.dma_start(slot(p_head)[:, 1024:1024 + P], w_kvb_v[:, bass.ds(h * (NOPE + VD), NOPE + VD)]).then_inc(
                    raw_in[p_head % 2], 16)
                load(p_head + 1, h * 2, k_major(p_head + 1, KD), w_in_v[:, :, bass.ds(h * 256 + C_G, 256)])
            sync.wait_ge(scan_done, 2)
            sync.dma_start(xt[:, :, :], x_v).then_inc(x_back, 16)
            for n, src in enumerate((w_ol_v, w_oa_v, w_ol_v, w_oa_v)):
                load(T_R // 2 + n, 0, k_major(T_R // 2 + n, 4), src[:, :, 512 * (n // 2):512 * (n // 2) + 512])
            for n in range(4):
                load(T_OUT // 2 + n, 0, k_major(T_OUT // 2 + n, 4),
                     w_out_v[:, 4 * (n % 2):4 * (n % 2) + 4, 512 * (n // 2):512 * (n // 2) + 512])
            p_ffn = T_FFN // 2
            with sync.Fori(0, FT // 2) as i:
                load(p_ffn, i * 2, k_major(p_ffn, KD), w_fg_v[:, :, bass.ds(i * 256, 256)])
                load(p_ffn + 1, i * 2, k_major(p_ffn + 1, KD), w_fu_v[:, :, bass.ds(i * 256, 256)])
            p_dn = T_DN // 2
            with sync.Fori(0, FT // 4) as i:
                for j in range(2):
                    load(p_dn + j, i * 2, k_major(p_dn + j, 2), w_fd_v[:, bass.ds(i * 4 + 2 * j, 2), :])
            load(p_dn + FT // 2 - 1, 0, k_major(p_dn + FT // 2 - 1, 2), w_fd_v[:, FT - 2:FT, :])
            for t in range(NT):
                sync.wait_ge(fin_ready, t + 1)
                sync.dma_start(out_v[:, t, :], xt[:, t, :]).then_inc(stored, 16)
            sync.wait_ge(stored, 16 * NT)

        @block.gpsimd
        def _(pool):
            nc.gpsimd.memset(ident[:, :], 0.0).then_inc(s_ident, 1)
            pool.wait_ge(s_ident, 1)
            nc.gpsimd.affine_select(out=ident[:, :], in_=ident[:, :], compare_op=ALU.not_equal, fill=1.0,
                                    base=0, pattern=[[-1, P]], channel_multiplier=1).then_inc(s_ident, 1)
            nc.gpsimd.memset(xp[:, :, 0:LEFT], 0.0)
            nc.gpsimd.memset(xp[:, :, LEFT + SEQ:], 0.0).then_inc(s_pad, 1)

            vs = f_hi[:, FV, :].rearrange("p (t c) -> p t c", t=NT)
            pool.wait_ge(v_ready, NT)

            def head(h):
                pool.wait_ge(q_prod, h + 1)
                nc.gpsimd.tensor_tensor(q_f[NOPE:QK, :], q_f[NOPE:QK, :], q_s[NOPE:QK, :], ALU.add).then_inc(q_full, 1)
                pool.wait_ge(q_half, h + 1)
                nc.gpsimd.tensor_tensor(f_lo[0:QK, FQ, :], q_f[0:QK, :], f_hi[0:QK, FQ, :].bitcast(F32),
                                        ALU.subtract).then_inc(q_ready, 1)
                pool.wait_ge(q_ready, h + 1)
                nc.gpsimd.tensor_copy(vs[:, :, 0:VD], val[:, :, bass.ds(h * VD, VD)]).then_inc(vs_half, 1)

            with pool.Fori(0, HEADS) as h:
                head(h)

        @block.scalar
        def _(act):
            def row_load(r, src):
                n = src.shape[0]
                act.dma_start(rows[r:r + n, :], src).then_inc(prm_in, 16)
            row_load(ROW_G1, norm1_g[0].rearrange("(n p) -> n p", p=P))
            row_load(ROW_GQ, q_a_norm_g[0].rearrange("(n p) -> n p", p=P))
            row_load(ROW_GKV, kv_a_norm_g[0].rearrange("(n p) -> n p", p=P))
            row_load(ROW_CW, conv_w[0].rearrange("j (n p) -> (j n) p", p=P))
            row_load(ROW_CB, conv_b[0].rearrange("(n p) -> n p", p=P))
            row_load(ROW_BR, b_rgate[0].rearrange("r n p -> (r n) p"))
            row_load(ROW_BI, b_igate[0].rearrange("r n p -> (r n) p"))
            row_load(ROW_LAM, lru_lambda[0].rearrange("r (n p) -> (r n) p", p=P))
            row_load(ROW_G2, norm2_g[0].rearrange("(n p) -> n p", p=P))
            act.dma_start(tab_q[:, :], rope_q).then_inc(tab_in, 16)
            act.dma_start(tab_k[:, :, :, :], rope_k).then_inc(tab_in, 16)
            act.dma_start(fin_g[:, :], final_g.rearrange("(a n) -> a n", a=1).to_broadcast([P, D])).then_inc(fin_in, 16)

            sums = [0]

            def square_sum(src, r, t, junk, back=1):
                if sums[0] > back:
                    act.wait_ge(ssq_ready, sums[0] - back)
                sums[0] += 1
                nc.scalar.activation(junk, src, ACT.Square, accum_out=ssq[:, r, t:t + 1]).then_inc(ssq_ready, 1)

            def root(r, t, n, count):
                act.wait_ge(rms_ready, count)
                nc.scalar.activation(rstd[:, r, t:t + n], rms[:, r, t:t + n], ACT.Sqrt).then_inc(rstd_ready, 1)

            for t in range(NT):
                act.wait_ge(x_in[t], 16)
                square_sum(xt[:, t, :], 0, t, sq_junk[:, t % 2, :])
                if t >= 1:
                    root(0, t - 1, 1, t)
            root(0, NT - 1, 1, NT)

            act.wait_ge(prm_ready, 1)
            split_hi(act, 0)
            for d in range(KD):
                act.wait_ge(xT_done, d + 1)
                nc.scalar.activation(hT_hi[:, d, :], ps[:, d, :], ACT.Copy,
                                     scale=prm[:, ROW_G1 + d:ROW_G1 + d + 1]).then_inc(h_half, 1)
                if d in (3, 5, 7):
                    split_hi(act, (d - 1) // 2)
            act.wait_ge(lam_neg, 1)
            nc.scalar.activation(sp[:, 1, :], sp[:, 0, :], ACT.Exp).then_inc(lam_exp, 1)
            act.wait_ge(s_pad, 1)
            for n in range(NB):
                tile_used(act, T_X + n)
                nc.scalar.activation(xp[:, n, LEFT:LEFT + SEQ], ps[:, n, :], ACT.Copy).then_inc(xp_ready, 1)
                split_hi(act, T_A + n)
            for n in range(NB):
                act.wait_ge(xc_full, n + 1)
                nc.scalar.activation(f_hi[:, FXC + n, :], xc[:, n, :], ACT.Copy).then_inc(xc_half, 1)
                if n == 0:
                    split_hi(act, T_G0)
                if n in (2, 3):
                    split_hi(act, T_Y + n - 2)
            for t in range(NT):
                a_done_wait(act, t)
                nc.scalar.activation(pa[:, t, :], ps[:, 4 + t, 0:CA], ACT.Copy).then_inc(pa_ready, 1)
                square_sum(ps[:, 4 + t, 0:QL], 1, t, sq_junk[:, 0, 0:QL])
                square_sum(ps[:, 4 + t, QL:QL + KVL], 1, NT + t, sq_junk[:, 1, 0:KVL])

            def gate_sigmoids(d, part):
                for n in range(NB):
                    gates_done(act, d, part, n)
                    b = (4 if d and not part else 0) + n
                    col = (ROW_BI if part else ROW_BR) + NB * d + n
                    nc.scalar.activation((lru_i if part else lru_r)[:, n, :], ps[:, b, :], ACT.Sigmoid,
                                         bias=prm[:, col:col + 1]).then_inc(sig_ready, 1)

            gate_sigmoids(0, 0)
            root(1, 0, 2 * NT, NT + 1)
            gate_sigmoids(0, 1)
            act.wait_ge(aT_done, 1)
            for m in range(3):
                act.wait_ge(aT_done, m + 1)
                nc.scalar.activation(f_hi[:, FQA + m, :], ps[:, 4 + m, :], ACT.Copy,
                                     scale=prm[:, ROW_GQ + m:ROW_GQ + m + 1]).then_inc(aT_half, 1)
            act.wait_ge(aT_done, 4)
            nc.scalar.activation(f_hi[NOPE:QK, FK, :], ps[NOPE:QK, 7, :], ACT.Copy).then_inc(aT_half, 1)
            split_hi(act, T_Y + 2)

            def decays(d):
                for n in range(NB):
                    col = NB * d + n
                    nc.scalar.activation(lru_a[:, n, :], lru_r[:, n, :], ACT.Exp, scale=decay[:, 1, col:col + 1])
                    nc.scalar.activation(lru_t[:, n, :], lru_r[:, n, :], ACT.Tanh, scale=decay[:, 0, col:col + 1])
                    nc.scalar.activation(lru_r[:, n, :], lru_r[:, n, :], ACT.Exp,
                                         scale=decay[:, 2, col:col + 1]).then_inc(exp3_ready, 1)

            def multipliers(d):
                act.wait_ge(m2_ready, d + 1)
                nc.scalar.activation(lru_r, lru_r, ACT.Sqrt).then_inc(mult_ready, 1)

            act.wait_ge(decay_ready, 3)
            act.wait_ge(sig_ready, 8)
            act.wait_ge(pa_norm, 4)
            act.wait_ge(aT_done, 4)
            decays(0)
            split_hi(act, T_Y + 3)
            multipliers(0)
            for m in range(NB):
                tile_used(act, T_Y + m)
                nc.scalar.activation(lru_y[:, m, :], ps[:, m, :], ACT.Gelu_apprx_tanh).then_inc(y_ready, 1)
                if m == 0:
                    split_hi(act, T_G1)
                if m == 1:
                    split_hi(act, T_V)
                if m == 2:
                    split_hi(act, T_HEAD)
                if m == 3:
                    split_hi(act, T_HEAD + 1)
            act.wait_ge(scan_done, 1)
            gate_sigmoids(1, 0)
            gate_sigmoids(1, 1)
            for t in range(NT):
                v_done_wait(act, t)
                nc.scalar.activation(val[:, t, :], ps[:, 4 + t, :], ACT.Copy).then_inc(v_ready, 1)
            split_hi(act, T_HEAD + 2)
            split_hi(act, T_HEAD + 3)
            act.wait_ge(sig_ready, 16)
            decays(1)
            multipliers(1)

            def head(h, h0):
                t0, dt = T_HEAD + 4 * h0 + 4, (h - h0) * 4
                tile_used(act, h * 4 + T_HEAD + 1)
                nc.scalar.activation(f_hi[0:NOPE, FK, :], ps[0:NOPE, 1, :], ACT.Copy).then_inc(k_half, 1)
                act.wait_ge(q_full, h + 1)
                nc.scalar.activation(f_hi[0:QK, FQ, :], q_f[0:QK, :], ACT.Copy).then_inc(q_half, 1)
                split_hi(act, t0, dt)
                split_hi(act, t0 + 1, dt)
                for t in range(NT):
                    act.wait_ge(nb_ready, h * 2 + t // 2 + 1)
                    nc.scalar.activation(prob[:, t, :], ps[:, 4 + t, :], ACT.Exp, bias=nbias[:, t:t + 1], scale=SCALE,
                                         accum_out=psum_p[:, t:t + 1]).then_inc(e_ready, 1)
                tile_used(act, h * 4 + T_HEAD + 2)
                nc.scalar.activation(store[:, h * 2, :], ps[:, 2, :], ACT.Copy).then_inc(gl_ready, 1)
                split_hi(act, t0 + 2, dt)
                for kt in range(NT):
                    act.wait_ge(t_done, h * 4 + kt + 1)
                    if kt >= 2:
                        act.wait_ge(pv_done, h * 4 + kt - 1)
                    nc.scalar.activation(f_hi[:, FPT + kt % 2, :], ps[:, 4 + kt, :], ACT.Copy).then_inc(pt_half, 1)
                tile_used(act, h * 4 + T_HEAD + 3)
                nc.scalar.activation(store[:, h * 2 + 1, :], ps[:, 3, :], ACT.Copy).then_inc(gl_ready, 1)
                split_hi(act, t0 + 3, dt)
                act.wait_ge(pv_done, h * 4 + 4)
                nc.scalar.activation(o_half[0:VD, :], ps[VD:P, 1, :], ACT.Copy).then_inc(oc_ready, 1)

            act.wait_ge(scan_done, 2)
            with act.Fori(0, HEADS - 1) as h:
                head(h, 0)
            head(HEADS - 1, HEADS - 1)

            act.wait_ge(rec_full, 1)
            for n in range(NB):
                nc.scalar.activation(f_hi[:, FREC + n, :], lru_h[:, n, :], ACT.Copy).then_inc(rec_half, 1)
            act.wait_ge(o_ready, HEADS + 1)
            for n in range(NB):
                nc.scalar.activation(f_hi[:, FO + n, :], o_t[:, n, :], ACT.Copy).then_inc(ot_half, 1)
            act.wait_ge(gl_ready, 2 * HEADS + 2)
            for g in (2, 0, 3, 1):
                nc.scalar.activation(store[:, 4 * g:4 * g + 4, :], store[:, 4 * g:4 * g + 4, :],
                                     ACT.Sigmoid).then_inc(gs_ready, 1)
            for n in range(4):
                split_hi(act, T_R + 4 + n)
            for m in range(KD):
                act.wait_ge(mg_full, m + 1)
                nc.scalar.activation(hT_hi[:, m, :], store[:, m, :], ACT.Copy).then_inc(mg_half, 1)
                for t in {3: (0, 1), 4: (2,), 6: (3,)}.get(m, ()):
                    split_hi(act, T_OUT + t)

            for t in range(4):
                split_hi(act, T_OUT + 4 + t)
            for t in range(NT):
                act.wait_ge(x2_ready, NT + t + 1)
                square_sum(xt[:, t, :], 2, t, sq_junk[:, t % 2, :])
                split_hi(act, T_FFN + t)
                root(2, t, 1, NT + 2 + t)
            for d in range(KD):
                act.wait_ge(xT_done, KD + d + 1)
                nc.scalar.activation(hT_hi[:, d, :], ps[:, d, :], ACT.Copy,
                                     scale=prm[:, ROW_G2 + d:ROW_G2 + d + 1]).then_inc(h2_half, 1)

            act.sem_inc(silu_ready, 2)

            def act_hi(n0, dn=0):
                act.wait_ge(act_ready, dn + n0 + 3)
                nc.scalar.activation(f_hi[:, FACT + n0 % 4, :], store[:, dn + n0, :], ACT.Copy).then_inc(act_half, 1)

            def ffn(i, i0):
                for j in range(2):
                    tile_used(act, i * 4 + T_FFN + j)
                    act.wait_ge(act_ready, i * 2 + j + 1)
                    nc.scalar.activation(silu[:, j, :], ps[:, j, :], ACT.Silu).then_inc(silu_ready, 1)
                    split_hi(act, T_FFN + 4 * i0 + 4 + j, (i - i0) * 4)
                    if i0:
                        act_hi(j)
                for j in range(2, 4):
                    split_hi(act, T_FFN + 4 * i0 + 4 + j, (i - i0) * 4)
                    if i0:
                        act_hi(j)

            with act.Fori(0, FT // 2 - 1) as i:
                ffn(i, 0)
            ffn(FT // 2 - 1, FT // 2 - 1)

            with act.Fori(0, 4) as i:
                for j in range(4):
                    split_hi(act, T_DN + 4 + j, i * 4)
                    act_hi(4 + j, i * 4)
            for n in (FT - 2, FT - 1):
                split_hi(act, T_DN + n)
                act_hi(n)

            for t in range(NT):
                act.wait_ge(y2_ready, t + 1)
                square_sum(xt[:, t, :], 3, t, sq_junk[:, t % 2, :])
                root(3, t, 1, 2 * NT + 2 + t)

        @block.vector
        def _(dve):
            steps = [0]

            def link(ins):
                steps[0] += 1
                ins.then_inc(dve_step, 1)
                dve.wait_ge(dve_step, steps[0])

            def inv_mean(r, t, n, width, ssq_count):
                dve.wait_ge(ssq_ready, ssq_count)
                link(nc.vector.tensor_scalar(rms[:, r, t:t + n], ssq[:, r, t:t + n], 1.0 / width, EPS, ALU.mult, ALU.add))

            def norm_tile(r, t, dst, ssq_count, rms_count):
                inv_mean(r, t, 1, D, ssq_count)
                nc.vector.reciprocal(rms[:, r, t:t + 1], rms[:, r, t:t + 1]).then_inc(rms_ready, 1)
                dve.wait_ge(rstd_ready, rms_count)
                nc.vector.tensor_scalar(dst, xt[:, t, :], rstd[:, r, t:t + 1], None, ALU.mult).then_inc(xn_ready, 1)

            dve.wait_ge(prm_t, 1)
            nc.vector.tensor_copy(prm[:, 0:N_ROWS], ps[:, 7, 0:N_ROWS]).then_inc(prm_ready, 1)
            dve.wait_ge(prm_ready, 1)
            lam = prm[:, ROW_LAM:ROW_LAM + 8]
            nc.vector.scalar_tensor_tensor(sp[:, 0, :], lam, -1.0, lam, ALU.mult, ALU.min).then_inc(lam_neg, 1)
            for t in range(NT):
                norm_tile(0, t, xt[:, t, :], t + 1, t + 1)
            split_lo(dve, 0)
            for d in range(KD):
                dve.wait_ge(h_half, d + 1)
                nc.vector.scalar_tensor_tensor(hT_lo[:, d, :], ps[:, d, :], prm[:, ROW_G1 + d:ROW_G1 + d + 1],
                                               hT_hi[:, d, :].bitcast(F32), ALU.mult, ALU.subtract).then_inc(h_ready, 1)
                if d in (3, 5, 7):
                    split_lo(dve, (d - 1) // 2)

            dve.wait_ge(lam_exp, 1)
            e, s, s2, q, r = (sp[:, k, :] for k in (1, 2, 3, 4, 5))
            link(nc.vector.tensor_scalar(r, e, 2.0, None, ALU.add))
            link(nc.vector.reciprocal(r, r))
            link(nc.vector.tensor_tensor(s, e, r, ALU.mult))
            link(nc.vector.tensor_tensor(s2, s, s, ALU.mult))
            link(nc.vector.tensor_scalar(q, s2, 1.0 / 17, None, ALU.mult))
            for k in (15, 13, 11, 9, 7, 5, 3):
                link(nc.vector.scalar_tensor_tensor(q, q, 1.0 / k, s2, ALU.add, ALU.mult))
            link(nc.vector.scalar_tensor_tensor(q, q, 1.0, s, ALU.add, ALU.mult))
            link(nc.vector.tensor_scalar(r, lam, -1.0, 0.0, ALU.mult, ALU.max))
            link(nc.vector.scalar_tensor_tensor(q, q, 2.0, r, ALU.mult, ALU.add))
            for k, f in enumerate((LRU_C, -LRU_C, -2 * LRU_C)):
                nc.vector.tensor_scalar(decay[:, k, :], q, f, None, ALU.mult).then_inc(decay_ready, 1)

            for n in range(NB):
                dve.wait_ge(xp_ready, n + 1)
                tap = [prm[:, ROW_CW + NB * j + n:ROW_CW + NB * j + n + 1] for j in range(TAPS)]
                link(nc.vector.tensor_scalar(xc[:, n, :], xp[:, n, 0:SEQ], tap[0], prm[:, ROW_CB + n:ROW_CB + n + 1],
                                             ALU.mult, ALU.add))
                for j in range(1, TAPS):
                    ins = nc.vector.scalar_tensor_tensor(xc[:, n, :], xp[:, n, j:j + SEQ], tap[j], xc[:, n, :],
                                                         ALU.mult, ALU.add)
                    if j < TAPS - 1:
                        link(ins)
                    else:
                        ins.then_inc(xc_full, 1)
                split_lo(dve, T_A + n)
            for n in range(NB):
                dve.wait_ge(xc_half, n + 1)
                nc.vector.tensor_tensor(f_lo[:, FXC + n, :], xc[:, n, :], f_hi[:, FXC + n, :].bitcast(F32),
                                        ALU.subtract).then_inc(xc_ready, 1)
                if n == 0:
                    split_lo(dve, T_G0)
                if n in (2, 3):
                    split_lo(dve, T_Y + n - 2)

            inv_mean(1, 0, NT, QL, 3 * NT)
            inv_mean(1, NT, NT, KVL, 3 * NT)
            nc.vector.reciprocal(rms[:, 1, :], rms[:, 1, :]).then_inc(rms_ready, 1)
            dve.wait_ge(tab_in, 32)
            dve.wait_ge(pa_ready, NT)
            k1, k2 = pa[:, :, QL + KVL:QL + KVL + HALF], pa[:, :, QL + KVL + HALF:CA]
            cos, sin = tab_k[:, :, 0, :], tab_k[:, :, 1, :]
            for dst, a, b in ((0, k1, cos), (1, k2, sin), (2, k2, cos)):
                nc.vector.tensor_tensor(ksc[:, dst, :, :], a, b, ALU.mult)
            link(nc.vector.tensor_tensor(ksc[:, 3, :, :], k1, sin, ALU.mult))
            nc.vector.tensor_tensor(k1, ksc[:, 0, :, :], ksc[:, 1, :, :], ALU.subtract)
            nc.vector.tensor_tensor(k2, ksc[:, 2, :, :], ksc[:, 3, :, :], ALU.add)
            dve.wait_ge(rstd_ready, NT + 1)
            for t in range(NT):
                nc.vector.tensor_scalar(pa[:, t, 0:QL], pa[:, t, 0:QL], rstd[:, 1, t:t + 1], None, ALU.mult)
                nc.vector.tensor_scalar(pa[:, t, QL:QL + KVL], pa[:, t, QL:QL + KVL], rstd[:, 1, NT + t:NT + t + 1],
                                        None, ALU.mult).then_inc(pa_norm, 1)
            for m in range(3):
                dve.wait_ge(aT_half, m + 1)
                nc.vector.scalar_tensor_tensor(f_lo[:, FQA + m, :], ps[:, 4 + m, :], prm[:, ROW_GQ + m:ROW_GQ + m + 1],
                                               f_hi[:, FQA + m, :].bitcast(F32), ALU.mult, ALU.subtract).then_inc(aT_ready, 1)
            dve.wait_ge(aT_half, 4)
            nc.vector.tensor_tensor(f_lo[NOPE:QK, FK, :], ps[NOPE:QK, 7, :], f_hi[NOPE:QK, FK, :].bitcast(F32),
                                    ALU.subtract).then_inc(aT_ready, 1)
            split_lo(dve, T_Y + 2)

            def recurrence(d):
                dve.wait_ge(sig_ready, 8 * d + 8)
                link(nc.vector.tensor_tensor(lru_i, lru_i, xc, ALU.mult))
                dve.wait_ge(exp3_ready, NB * (d + 1))
                nc.vector.scalar_tensor_tensor(lru_r, lru_r, 1.0, lru_t, ALU.add, ALU.mult).then_inc(m2_ready, 1)
                if d == 0:
                    split_lo(dve, T_Y + 3)
                dve.wait_ge(mult_ready, d + 1)
                link(nc.vector.tensor_tensor(lru_i, lru_i, lru_r, ALU.mult))
                for n in range(NB):
                    if d == 0:
                        ins = nc.vector.tensor_tensor_scan(lru_h[:, n, :], lru_a[:, n, :], lru_i[:, n, :], 0.0,
                                                           ALU.mult, ALU.add)
                    else:
                        ins = nc.vector.tensor_tensor_scan(lru_t[:, n, ::-1], lru_a[:, n, ::-1], lru_i[:, n, ::-1], 0.0,
                                                           ALU.mult, ALU.add)
                return ins

            recurrence(0).then_inc(scan_done, 1)
            split_lo(dve, T_G1)
            split_lo(dve, T_V)
            split_lo(dve, T_HEAD)
            split_lo(dve, T_HEAD + 1)
            split_lo(dve, T_HEAD + 2)
            split_lo(dve, T_HEAD + 3)
            link(recurrence(1))
            link(nc.vector.tensor_tensor(lru_h[:, :, :], lru_h[:, :, :], lru_t, ALU.add))
            nc.vector.sem_inc(scan_done, 1)
            dve.wait_ge(y_ready, NB)
            nc.vector.tensor_tensor(lru_h[:, :, :], lru_h[:, :, :], lru_y[:, :, :], ALU.mult).then_inc(rec_full, 1)

            nc.vector.sem_inc(o_ready, 1)
            nc.vector.sem_inc(gl_ready, 2)

            vs = f_hi[:, FV, :].rearrange("p (t c) -> p t c", t=NT)

            def head(h, h0, out_slice):
                t0, dt = T_HEAD + 4 * h0 + 4, (h - h0) * 4
                tile_used(dve, h * 4 + T_HEAD)
                nc.vector.tensor_tensor(q_f[0:QK, :], ps[0:QK, 0, :], tab_q[0:QK, :], ALU.mult)
                nc.vector.tensor_tensor(q_s[NOPE:QK, :], ps[QK:P, 0, :], tab_q[QK:P, :], ALU.mult).then_inc(q_prod, 1)
                dve.wait_ge(k_half, h + 1)
                nc.vector.tensor_tensor(f_lo[0:NOPE, FK, :], ps[0:NOPE, 1, :], f_hi[0:NOPE, FK, :].bitcast(F32),
                                        ALU.subtract).then_inc(k_ready, 1)
                split_lo(dve, t0, dt)
                split_lo(dve, t0 + 1, dt)
                dve.wait_ge(vs_half, h + 1)
                nc.vector.tensor_tensor(vs[:, :, VD:P], val[:, :, bass.ds(h * VD, VD)], vs[:, :, 0:VD].bitcast(F32),
                                        ALU.subtract).then_inc(vs_ready, 1)
                for c in range(2):
                    dve.wait_ge(sc_done, h * 4 + 2 * c + 2)
                    nc.vector.reduce_max(mx[:, 2 * c:2 * c + 2], ps[:, 4 + 2 * c:6 + 2 * c, :], AX_X).then_inc(max_ready, 1)
                    dve.wait_ge(max_ready, h * 2 + c + 1)
                    nc.vector.tensor_scalar(nbias[:, 2 * c:2 * c + 2], mx[:, 2 * c:2 * c + 2], -SCALE, None,
                                            ALU.mult).then_inc(nb_ready, 1)
                for t in range(NT):
                    dve.wait_ge(e_ready, h * 4 + t + 1)
                    nc.vector.reciprocal(rsum[:, t:t + 1], psum_p[:, t:t + 1]).then_inc(rs_ready, 1)
                    dve.wait_ge(rs_ready, h * 4 + t + 1)
                    nc.vector.tensor_scalar(prob[:, t, :], prob[:, t, :], rsum[:, t:t + 1], None, ALU.mult).then_inc(p_ready, 1)
                split_lo(dve, t0 + 2, dt)
                for kt in range(NT):
                    dve.wait_ge(pt_half, h * 4 + kt + 1)
                    nc.vector.tensor_tensor(f_lo[:, FPT + kt % 2, :], ps[:, 4 + kt, :], f_hi[:, FPT + kt % 2, :].bitcast(F32),
                                            ALU.subtract).then_inc(pt_ready, 1)
                split_lo(dve, t0 + 3, dt)
                dve.wait_ge(oc_ready, h + 1)
                nc.vector.tensor_tensor(out_slice, ps[0:VD, 1, :], o_half[0:VD, :], ALU.add).then_inc(o_ready, 1)

            with dve.Fori(0, HEADS // 2 - 1) as i:
                for j in range(2):
                    head(i * 2 + j, 0, o_t[VD * j:VD * j + VD, i, :])
            for h in (HEADS - 2, HEADS - 1):
                head(h, h if h == HEADS - 1 else 0, o_t[VD * (h % 2):VD * (h % 2) + VD, h // 2, :])

            for n in range(NB):
                dve.wait_ge(rec_half, n + 1)
                nc.vector.tensor_tensor(f_lo[:, FREC + n, :], lru_h[:, n, :], f_hi[:, FREC + n, :].bitcast(F32),
                                        ALU.subtract).then_inc(rec_ready, 1)
            for n in range(NB):
                dve.wait_ge(ot_half, n + 1)
                nc.vector.tensor_tensor(f_lo[:, FO + n, :], o_t[:, n, :], f_hi[:, FO + n, :].bitcast(F32),
                                        ALU.subtract).then_inc(ot_ready, 1)
            for half in range(2):
                for m in range(4 * half, 4 * half + 4):
                    branch_done(dve, rl_done, 0, m)
                    dve.wait_ge(gs_ready, 2 * half + 1)
                    nc.vector.tensor_tensor(store[:, KD + m, :], ps[:, m % 4, :], store[:, KD + m, :],
                                            ALU.mult).then_inc(rl_gated, 1)
                    if m % 2 == 0:
                        split_lo(dve, T_R + 4 * half + 4 + m % 4 // 2) if not half else split_lo(dve, T_OUT + m % 4 // 2)
                for m in range(4 * half, 4 * half + 4):
                    branch_done(dve, ra_done, 1, m)
                    dve.wait_ge(gs_ready, 2 * half + 2)
                    nc.vector.tensor_tensor(store[:, m, :], ps[:, 4 + m % 4, :], store[:, m, :],
                                            ALU.mult).then_inc(ra_gated, 1)
                    dve.wait_ge(ra_gated, m + 1)
                    dve.wait_ge(rl_gated, m + 1)
                    nc.vector.tensor_tensor(store[:, m, :], store[:, m, :], store[:, KD + m, :], ALU.add).then_inc(mg_full, 1)
                    dve.wait_ge(mg_half, m + 1)
                    nc.vector.tensor_tensor(hT_lo[:, m, :], store[:, m, :], hT_hi[:, m, :].bitcast(F32),
                                            ALU.subtract).then_inc(mg_ready, 1)
                    if m % 2 == 0:
                        split_lo(dve, T_R + 4 * half + 6 + m % 4 // 2) if not half else split_lo(dve, T_OUT + 2 + m % 4 // 2)
            for t in range(4):
                split_lo(dve, T_OUT + 4 + t)

            dve.wait_ge(x_back, 16)
            for c in range(2):
                for t in range(NT):
                    w_out_done(dve, c, t)
                    part = xt[:, t, 512 * c:512 * c + 512]
                    nc.vector.tensor_tensor(part, part, ps[:, 4 * c + t, :], ALU.add).then_inc(x2_ready, 1)
                    if c == 1:
                        split_lo(dve, T_FFN + t)
                        norm_tile(2, t, xn[:, t, :], 3 * NT + t + 1, NT + 2 + t)
            for d in range(KD):
                dve.wait_ge(h2_half, d + 1)
                nc.vector.scalar_tensor_tensor(hT_lo[:, d, :], ps[:, d, :], prm[:, ROW_G2 + d:ROW_G2 + d + 1],
                                               hT_hi[:, d, :].bitcast(F32), ALU.mult, ALU.subtract).then_inc(h2_ready, 1)

            nc.vector.sem_inc(act_ready, 2)

            def act_lo(n0, dn=0):
                dve.wait_ge(act_half, dn + n0 + 1)
                nc.vector.tensor_tensor(f_lo[:, FACT + n0 % 4, :], store[:, dn + n0, :],
                                        f_hi[:, FACT + n0 % 4, :].bitcast(F32), ALU.subtract).then_inc(act_split, 1)

            def ffn(i, i0):
                for j in range(2):
                    split_lo(dve, T_FFN + 4 * i0 + 4 + j, (i - i0) * 4)
                    if i0:
                        act_lo(j)
                for j in range(2):
                    dve.wait_ge(silu_ready, i * 2 + j + 3)
                    tile_used(dve, i * 4 + T_FFN + 2 + j)
                    nc.vector.tensor_tensor(store[:, i * 2 + j, :], silu[:, j, :], ps[:, 2 + j, :],
                                            ALU.mult).then_inc(act_ready, 1)
                    split_lo(dve, T_FFN + 4 * i0 + 6 + j, (i - i0) * 4)
                    if i0:
                        act_lo(2 + j)

            with dve.Fori(0, FT // 2 - 1) as i:
                ffn(i, 0)
            ffn(FT // 2 - 1, FT // 2 - 1)
            with dve.Fori(0, 4) as i:
                for j in range(4):
                    split_lo(dve, T_DN + 4 + j, i * 4)
                    act_lo(4 + j, i * 4)
            for n in (FT - 2, FT - 1):
                split_lo(dve, T_DN + n)
                act_lo(n)

            dve.wait_ge(fin_in, 16)
            for t in range(NT):
                dve.wait_ge(dn_done, t + 1)
                xr = xt[:, t, :].rearrange("p (c n) -> p c n", c=2)
                nc.vector.tensor_tensor(xr, xr, ps[:, 2 * t:2 * t + 2, :], ALU.add).then_inc(y2_ready, 1)
                inv_mean(3, t, 1, D, 4 * NT + t + 1)
                nc.vector.reciprocal(rms[:, 3, t:t + 1], rms[:, 3, t:t + 1]).then_inc(rms_ready, 1)
                dve.wait_ge(rstd_ready, 2 * NT + 2 + t)
                nc.vector.scalar_tensor_tensor(xt[:, t, :], xt[:, t, :], rstd[:, 3, t:t + 1], fin_g[:, :],
                                               ALU.mult, ALU.mult).then_inc(fin_ready, 1)

        @block.tensor
        def _(pe):
            def cols_tile(t0, dt, bank, ks=range(KD), h_sem=None):
                wh = split_view(w_hi, "cols", t0 % 4)
                wl = split_view(w_lo, "cols", t0 % 4)
                if 0 in ks:
                    pe.wait_ge(w_ready, dt + t0 + 1)
                for k in ks:
                    if h_sem is not None:
                        pe.wait_ge(h_sem, k + 1)
                    last = product(ps[:, bank, :], wh[:, k, :], wl[:, k, :], hT_hi[:, k, :], hT_lo[:, k, :],
                                   k == 0, k == KD - 1)
                return last

            def used(ins, n=1):
                ins.then_inc(w_used, n)

            pe.wait_ge(s_ident, 2)
            pe.wait_ge(prm_in, 16 * 9)
            nc.tensor.transpose(ps[:, 7, 0:N_ROWS], rows[0:N_ROWS, :], ident[0:N_ROWS, 0:N_ROWS]).then_inc(prm_t, 1)

            def transpose_norm(src, count):
                for t in range(NT):
                    pe.wait_ge(xn_ready, count + t + 1)
                    for d in range(KD):
                        ins = nc.tensor.transpose(ps[:, d, P * t:P * t + P], src[:, t, P * d:P * d + P], ident[:, :])
                        if t == NT - 1:
                            ins.then_inc(xT_done, 1)

            pe.wait_ge(prm_ready, 1)
            transpose_norm(xt, 0)

            for m in range(NB):
                used(cols_tile(T_X + m, 0, m, h_sem=h_ready if m == 0 else None))
            for n in range(4):
                t0 = T_A + n
                pe.wait_ge(w_ready, t0 + 1)
                wh, wl = split_view(w_hi, "a", t0 % 4), split_view(w_lo, "a", t0 % 4)
                for kk in range(2):
                    k = 2 * n + kk
                    for t in range(NT):
                        tok = slice(P * t, P * t + P)
                        last = product(ps[:, 4 + t, 0:CA], hT_hi[:, k, tok], hT_lo[:, k, tok], wh[:, kk, :], wl[:, kk, :],
                                       k == 0, k == KD - 1)
                        if k == KD - 1 and t < NT - 1:
                            last.then_inc(a_done, 1)
                used(last)

            def lru_gates(d, t0):
                pe.wait_ge(w_ready, t0 + tiles_in(t0))
                for part in range(2):
                    for n in range(NB):
                        if d == 0 and part == 0:
                            pe.wait_ge(xc_ready, n + 1)
                        if d == 0 and part == 1:
                            pe.wait_ge(sig_ready, n + 1)
                        if d == 1 and part == 1:
                            pe.wait_ge(y_ready, n + 1)
                        col = slice(512 * part + P * n, 512 * part + P * n + P)
                        b = (4 if d and not part else 0) + n
                        last = product(ps[:, b, :], w_hi[:, t0 % 4, col], w_lo[:, t0 % 4, col],
                                       f_hi[:, FXC + n, :], f_lo[:, FXC + n, :], True, True)
                        if not (part and n == NB - 1):
                            last.then_inc(g_done, 1)
                used(last, tiles_in(t0))

            pe.wait_ge(xp_ready, NB)
            lru_gates(0, T_G0)
            pe.wait_ge(pa_norm, NT)
            for m in range(4):
                lo, n = (P * m, P) if m < 3 else (CA - QK, QK)
                for t in range(NT):
                    ins = nc.tensor.transpose(ps[0:n, 4 + m, P * t:P * t + P], pa[:, t, lo:lo + n], ident[:, :])
                ins.then_inc(aT_done, 1)
            for m in range(NB):
                pe.wait_ge(sig_ready, NB + m + 1)
                used(cols_tile(T_Y + m, 0, m))
            pe.wait_ge(aT_ready, 4)
            lru_gates(1, T_G1)
            pe.wait_ge(w_ready, T_V + 1)
            for t in range(NT):
                pe.wait_ge(sig_ready, 8 + t + 1)
                tok = slice(P * t, P * t + P)
                last = product(ps[:, 4 + t, :], f_hi[:, FKVA, tok], f_lo[:, FKVA, tok],
                               w_hi[:, T_V % 4, 0:512], w_lo[:, T_V % 4, 0:512], True, True)
                if t < NT - 1:
                    last.then_inc(v_done, 1)
            used(last)

            vs = f_hi[:, FV, :].rearrange("p (t c) -> p t c", t=NT)

            def head(h):
                dt = h * 4
                pe.wait_ge(w_ready, dt + T_HEAD + 1)
                for k in range(2):
                    col = slice(P * k, P * k + P)
                    last = product(ps[:, 0, :], w_hi[:, 0, col], w_lo[:, 0, col], f_hi[:, FQA + k, :], f_lo[:, FQA + k, :],
                                   k == 0, k == 1)
                used(last)
                pe.wait_ge(w_ready, dt + T_HEAD + 2)
                pe.wait_ge(o_ready, h + 1)
                used(product(ps[:, 1, :], w_hi[:, 1, 0:P], w_lo[:, 1, 0:P], f_hi[:, FKVA, :], f_lo[:, FKVA, :], True, True))
                pe.wait_ge(gl_ready, h * 2 + 1)
                cols_tile(T_HEAD + 2, dt, 2, range(0, 4))
                pe.wait_ge(q_ready, h + 1)
                pe.wait_ge(k_ready, h + 1)
                for t in range(NT):
                    tok = slice(P * t, P * t + P)
                    product(ps[:, 4 + t, :], f_hi[0:QK, FQ, tok], f_lo[0:QK, FQ, tok], f_hi[0:QK, FK, :], f_lo[0:QK, FK, :],
                            True, True).then_inc(sc_done, 1)
                used(cols_tile(T_HEAD + 2, dt, 2, range(4, KD)))
                pe.wait_ge(gl_ready, h * 2 + 2)
                cols_tile(T_HEAD + 3, dt, 3, range(0, 4))
                pe.wait_ge(p_ready, h * 4 + 4)
                for kt in range(NT):
                    for t in range(NT):
                        ins = nc.tensor.transpose(ps[:, 4 + kt, P * t:P * t + P], prob[:, t, P * kt:P * kt + P], ident[:, :])
                    ins.then_inc(t_done, 1)
                used(cols_tile(T_HEAD + 3, dt, 3, range(4, KD)))
                pe.wait_ge(vs_ready, h + 1)
                for kt in range(NT):
                    pe.wait_ge(pt_ready, h * 4 + kt + 1)
                    both = lambda: nc.tensor.matmul(ps[:, 1, :], vs[:, kt, :], f_hi[:, FPT + kt % 2, :],
                                                    start=kt == 0, stop=kt == NT - 1)
                    p_lo = lambda: nc.tensor.matmul(ps[0:VD, 1, :], vs[:, kt, 0:VD], f_lo[:, FPT + kt % 2, :],
                                                    start=False, stop=False)
                    if kt == 0:
                        both()
                        p_lo().then_inc(pv_done, 1)
                    else:
                        p_lo()
                        both().then_inc(pv_done, 1)

            pe.wait_ge(sig_ready, 16)
            pe.wait_ge(v_ready, NT)
            with pe.Fori(0, HEADS) as h:
                head(h)

            pe.wait_ge(o_ready, HEADS + 1)
            pe.wait_ge(gl_ready, 2 * HEADS + 2)
            for half in range(2):
                for branch in range(2):
                    for j in range(2):
                        t0 = T_R + 4 * half + 2 * branch + j
                        pe.wait_ge(w_ready, t0 + 1)
                        wh, wl = split_view(w_hi, "wo", t0 % 4), split_view(w_lo, "wo", t0 % 4)
                        for c in range(2):
                            m = 4 * half + 2 * j + c
                            if half:
                                pe.wait_ge(ra_gated if branch else rl_gated, m - 3)
                            for k in range(4):
                                if not half and j == c == 0:
                                    pe.wait_ge(ot_ready if branch else rec_ready, k + 1)
                                f = (FO if branch else FREC) + k
                                last = product(ps[:, 4 * branch + m % 4, :], wh[:, k, P * c:P * c + P],
                                               wl[:, k, P * c:P * c + P], f_hi[:, f, :], f_lo[:, f, :], k == 0, k == 3)
                            if c == 0:
                                last.then_inc(ra_done if branch else rl_done, 1)
                        used(last)

            for n in range(8):
                t0, c = T_OUT + n, n // 4
                pe.wait_ge(w_ready, t0 + 1)
                for kk in range(2):
                    k = 2 * (n % 4) + kk
                    if c == 0:
                        pe.wait_ge(mg_ready, k + 1)
                    if k == 0:
                        pe.wait_ge(ra_gated if c else rl_gated, KD)
                    wcol = slice(512 * kk, 512 * kk + 512)
                    for t in range(NT):
                        tok = slice(P * t, P * t + P)
                        last = product(ps[:, 4 * c + t, :], hT_hi[:, k, tok], hT_lo[:, k, tok],
                                       w_hi[:, t0 % 4, wcol], w_lo[:, t0 % 4, wcol], k == 0, k == KD - 1)
                        if k == KD - 1 and t < NT - 1:
                            last.then_inc(wo_done, 1)
                used(last)

            pe.wait_ge(x2_ready, 2 * NT)
            transpose_norm(xn, NT)

            def ffn(i, first):
                for part in range(2):
                    for j in range(2):
                        pe.wait_ge(act_ready if part else silu_ready, i * 2 + j + 1)
                        used(cols_tile(T_FFN + 2 * part + j, i * 4, 2 * part + j,
                                       h_sem=h2_ready if first and part == j == 0 else None))

            ffn(0, True)
            with pe.Fori(1, FT // 2) as i:
                ffn(i, False)

            def down(n0, dn, toks, banks=2):
                pe.wait_ge(w_ready, dn + T_DN + n0 + 1)
                pe.wait_ge(act_split, dn + n0 + 1)
                for t in toks:
                    last = down_tok(n0, t)
                return last

            def down_tok(n0, t, stop=False):
                a, s = FACT + n0 % 4, n0 % 4
                tok = slice(P * t, P * t + P)
                for c in range(2):
                    last = product(ps[:, 2 * t + c, :], f_hi[:, a, tok], f_lo[:, a, tok],
                                   w_hi[:, s, 512 * c:512 * c + 512], w_lo[:, s, 512 * c:512 * c + 512], n0 == 0, stop)
                return last

            down(0, 0, (2, 3))
            pe.wait_ge(act_ready, FT + 2)
            pe.wait_ge(silu_ready, FT + 2)
            used(down(0, 0, (0, 1)))
            for n in (1, 2, 3):
                used(down(n, 0, range(NT)))
            with pe.Fori(0, 4) as i:
                for j in range(4):
                    used(down(4 + j, i * 4, range(NT)))
            pe.wait_ge(w_ready, T_DN + FT)
            pe.wait_ge(act_split, FT)
            for t in range(NT):
                down_tok(FT - 2, t)
                down_tok(FT - 1, t, stop=True).then_inc(dn_done, 1)


_INS = ["x", "norm1_g", "w_in", "q_a_norm_g", "w_q_b", "kv_a_norm_g", "w_kv_b", "w_o_attn", "conv_w", "conv_b",
        "w_rgate", "b_rgate", "w_igate", "b_igate", "lru_lambda", "w_o_lru", "w_out", "norm2_g", "w_ffn_gate",
        "w_ffn_up", "w_ffn_down", "final_g"]


def kernel(**inputs):
    import concourse.bacc as _bacc
    from concourse.bass_utils import run_bass_kernel_spmd as _run

    nc = _bacc.Bacc("TRN2", target_bir_lowering=False, num_devices=1, dynamic_dma_scratch_size=1024)
    arrays, args = {}, []
    tab_q, tab_k = rope_constants()
    for name, a in [(n, inputs[n]) for n in _INS] + [("rope_q", tab_q), ("rope_k", tab_k)]:
        a = np.ascontiguousarray(a)
        arrays[f"in_{name}_dram"] = a
        args.append(nc.dram_tensor(f"in_{name}_dram", a.shape, mybir.dt.from_np(a.dtype), kind="ExternalInput").ap())
    args.append(nc.dram_tensor("out_dram", (1, SEQ, D), F32, kind="ExternalOutput").ap())
    build(nc, *args)
    r = _run(nc, [arrays], core_ids=[0])
    return r.results[0]["out_dram"]
```

```python
from contextlib import ExitStack

import numpy as np

import concourse.bass as bass
from concourse import mybir

P = 128
ALU = mybir.AluOpType
ACT = mybir.ActivationFunctionType
AX_X = mybir.AxisListType.X
F32 = mybir.dt.float32
F32R = mybir.dt.float32r

D = 1024
SEQ = 512
KD = D // P
NT = SEQ // P
HEADS, NOPE, ROPE, VD = 8, 64, 32, 64
QK = NOPE + ROPE
HALF = ROPE // 2
QL, KVL = 256, 128
CA = QL + KVL + ROPE
W = 512
NB = W // P
TAPS, LEFT = 4, 2
LRU_C = 8.0
FF = 2816
FT = FF // P
EPS = 1e-6
SCALE = float(QK) ** -0.5
C_LX, C_LY, C_G = CA, CA + W, CA + 2 * W

T_X, T_A, T_G0, T_Y, T_V, T_G1 = 0, 4, 8, 10, 14, 15
T_HEAD = 16
T_R = T_HEAD + 4 * HEADS
T_OUT = T_R + 8
T_FFN = T_OUT + 8
T_DN = T_FFN + 2 * FT
PAIR_INC = 48

ROW_G1, ROW_G2, ROW_GQ, ROW_GKV, ROW_CW, ROW_CB, ROW_BR, ROW_BI, ROW_LAM = 0, 8, 16, 18, 19, 35, 39, 47, 55
N_ROWS = 63


def rope_constants():
    inv = (1.0 / (np.float32(10000.0) ** (np.arange(0, ROPE, 2, dtype=np.float32) / np.float32(ROPE)))).astype(np.float32)
    ang = np.arange(SEQ, dtype=np.float32)[:, None] * inv[None, :]
    cos, sin = np.cos(ang).astype(np.float32), np.sin(ang).astype(np.float32)
    q = np.concatenate([np.ones((NOPE, SEQ), np.float32), cos.T, cos.T, -sin.T, sin.T], axis=0)
    k = np.stack([cos, sin], axis=1).reshape(NT, P, 2, HALF).transpose(1, 0, 2, 3)
    return np.ascontiguousarray(q), np.ascontiguousarray(k)


def build(nc, x, norm1_g, w_in, q_a_norm_g, w_q_b, kv_a_norm_g, w_kv_b, w_o_attn, conv_w, conv_b,
          w_rgate, b_rgate, w_igate, b_igate, lru_lambda, w_o_lru, w_out, norm2_g, w_ffn_gate,
          w_ffn_up, w_ffn_down, final_g, rope_q, rope_k, out):
    x_v = x[0].rearrange("(t p) n -> p t n", p=P)
    out_v = out[0].rearrange("(t p) n -> p t n", p=P)
    w_in_v = w_in[0].rearrange("(k p) n -> p k n", p=P)
    w_qb_v = w_q_b[0].rearrange("(k p) n -> p k n", p=P)
    w_kvb_v = w_kv_b[0]
    w_val_v = w_kv_b[0].rearrange("p (h a c) -> p h a c", a=2, c=VD)
    w_r_v = w_rgate[0].rearrange("r n c d -> c r n d")
    w_i_v = w_igate[0].rearrange("r n c d -> c r n d")
    w_ol_v = w_o_lru[0].rearrange("(k p) n -> p k n", p=P)
    w_oa_v = w_o_attn[0].rearrange("(k p) n -> p k n", p=P)
    w_out_v = w_out[0].rearrange("(k p) n -> p k n", p=P)
    w_fg_v = w_ffn_gate[0].rearrange("(k p) n -> p k n", p=P)
    w_fu_v = w_ffn_up[0].rearrange("(k p) n -> p k n", p=P)
    w_fd_v = w_ffn_down[0].rearrange("(k p) n -> p k n", p=P)

    with ExitStack() as ctx:
        def sb(name, shape, dt=F32):
            return ctx.enter_context(nc.sbuf_tensor(name, shape, dt))

        def sem(name):
            return ctx.enter_context(nc.semaphore(name))

        ident = sb("ident", [P, P])
        rows = sb("rows", [64, P])
        prm = sb("prm", [P, 64])
        xt = sb("xt", [P, NT, D])
        hT_hi = sb("hT_hi", [P, KD, SEQ], F32R)
        hT_lo = sb("hT_lo", [P, KD, SEQ], F32R)
        raw = sb("raw", [P, 2, 2048])
        w_hi = sb("w_hi", [P, 4, 1024], F32R)
        w_lo = sb("w_lo", [P, 4, 1024], F32R)
        store = sb("store", [P, FT, SEQ])
        lru_hy = sb("lru_hy", [P, 2 * NB, SEQ])
        lru_h = lru_hy[:, 0:NB, :]
        lru_y = lru_hy[:, NB:2 * NB, :]
        yg = lru_hy
        val = sb("val", [P, NT, HEADS * VD])
        prob = sb("prob", [P, NT, SEQ])
        f_hi = sb("f_hi", [P, 8, SEQ], F32R)
        f_lo = sb("f_lo", [P, 8, SEQ], F32R)
        tab_q = sb("tab_q", [P, SEQ])
        tab_k = sb("tab_k", [P, NT, 2, HALF])
        fin_g = sb("fin_g", [P, D])
        ksc = sb("ksc", [P, 4, NT, HALF])
        nwt = sb("nwt", [P, 8])
        o_half = sb("o_half", [P, SEQ])
        lru_m = sb("lru_m", [P, SEQ])
        ssq = sb("ssq", [P, 4, 8])
        mse = sb("mse", [P, 4, 8])
        rms = sb("rms", [P, 4, 8])
        rstd = sb("rstd", [P, 4, 8])
        sp = sb("sp", [P, 8, 8])
        decay = sb("decay", [P, 3, 8])
        mx = sb("mx", [P, NT])
        nbias = sb("nbias", [P, NT])
        psum_p = sb("psum_p", [P, NT])
        rsum = sb("rsum", [P, NT])
        ps = ctx.enter_context(nc.psum_tensor("ps", [P, 8, SEQ], F32))

        FQA, FKVA, FK, FQ, FPT, FV = 0, 2, 3, 4, 5, 7
        FXC, FREC, FO, FACT = 4, 0, 4, 0

        xp = store[:, 0:5, :].rearrange("p a n -> p (a n)")[:, 0:NB * (SEQ + TAPS - 1)].rearrange(
            "p (n s) -> p n s", n=NB)
        pa = store[:, 5:9, 0:CA]
        xc = store[:, 16:20, :]
        o_t = store[:, 16:20, :]
        q_f, q_s = store[:, 20, :], store[:, 21, :]
        lru_r = [xt[:, 0:2, :].rearrange("p t (a n) -> p (t a) n", a=2), store[:, 8:12, :]]
        lru_i = [xt[:, 2:4, :].rearrange("p t (a n) -> p (t a) n", a=2), store[:, 12:16, :]]
        lru_a, lru_t = fin_g[:, 0:SEQ], fin_g[:, SEQ:2 * SEQ]
        xn = store[:, 0:8, :].rearrange("p (t a) n -> p t (a n)", a=2)
        sq_junk = prob[:, :, :].rearrange("p (t a) n -> p t (a n)", a=2)
        silu = prob[:, 0:2, :]

        x_in = [sem(f"x_in{t}") for t in range(NT)]
        x_back = sem("x_back")
        g1_in, prm_in, tab_in, fin_in = sem("g1_in"), sem("prm_in"), sem("tab_in"), sem("fin_in")
        raw_in = [sem("raw_in0"), sem("raw_in1")]
        w_half = sem("w_half")
        w_ready = sem("w_ready")
        w_used = sem("w_used")
        s_ident, s_pad = sem("ident_ready"), sem("pad_ready")
        prm_t, prm_ready = sem("prm_t"), sem("prm_ready")
        ssq_ready, rms_ready, rstd_ready = sem("ssq_ready"), sem("rms_ready"), sem("rstd_ready")
        xn_ready, xT_done, h_half, h_ready = sem("xn_ready"), sem("xT_done"), sem("h_half"), sem("h_ready")
        xp_ready, xc_full, xc_half, xc_ready = (
            sem("xp_ready"), sem("xc_full"), sem("xc_half"), sem("xc_ready"))
        a_done, pa_ready, pa_norm, aT_done, aT_half, aT_ready = (
            sem("a_done"), sem("pa_ready"), sem("pa_norm"), sem("aT_done"), sem("aT_half"), sem("aT_ready"))
        lam_neg, lam_exp, decay_ready = sem("lam_neg"), sem("lam_exp"), sem("decay_ready")
        g_done, sig_ready, exp3_ready, m2_ready, mult_ready, scan_done = (
            sem("g_done"), sem("sig_ready"), sem("exp3_ready"), sem("m2_ready"), sem("mult_ready"), sem("scan_done"))
        ixc_ready, u_ready, turned, hsum_ready = sem("ixc_ready"), sem("u_ready"), sem("turned"), sem("hsum_ready")
        y_ready, rec_full, rec_half, rec_ready = (
            sem("y_ready"), sem("rec_full"), sem("rec_half"), sem("rec_ready"))
        v_done, v_ready = sem("v_done"), sem("v_ready")
        q_prod, q_full, q_half, q_ready, k_half, k_ready = (
            sem("q_prod"), sem("q_full"), sem("q_half"), sem("q_ready"),
            sem("k_half"), sem("k_ready"))
        vs_half, vs_ready = sem("vs_half"), sem("vs_ready")
        sc_done, max_ready, nb_ready, e_ready, rs_ready, p_ready = (
            sem("sc_done"), sem("max_ready"), sem("nb_ready"), sem("e_ready"), sem("rs_ready"), sem("p_ready"))
        gl_ready = sem("gl_ready")
        t_done, pt_half, pt_ready, pv_done = sem("t_done"), sem("pt_half"), sem("pt_ready"), sem("pv_done")
        oc_ready, o_ready, ot_half, ot_ready = sem("oc_ready"), sem("o_ready"), sem("ot_half"), sem("ot_ready")
        rl_done, ra_done, rl_gated, ra_gated, mg_full, mg_half, mg_ready = (
            sem("rl_done"), sem("ra_done"), sem("rl_gated"), sem("ra_gated"), sem("mg_full"), sem("mg_half"),
            sem("mg_ready"))
        wo_done, x2_ready, h2_half, h2_ready = sem("wo_done"), sem("x2_ready"), sem("h2_half"), sem("h2_ready")
        silu_ready, act_ready = sem("silu_ready"), sem("act_ready")
        act_half, act_split = sem("act_half"), sem("act_split")
        dn_done, y2_ready, yg_ready, scale_ready, fin_left, fin_right, stored = (
            sem("dn_done"), sem("y2_ready"), sem("yg_ready"), sem("scale_ready"), sem("fin_left"), sem("fin_right"),
            sem("stored"))
        dve_step = sem("dve_step")
        block = ctx.enter_context(nc.Block())

        def raw_view(kind, slot, j):
            r = raw[:, slot, :]
            if kind == "cols":
                return r.rearrange("p (k n) -> p k n", k=KD)[:, :, P * j:P * j + P]
            if kind == "a":
                return r[:, 0:4 * CA].rearrange("p (k n) -> p k n", k=4)[:, 2 * j:2 * j + 2, :]
            if kind == "wo":
                return r.rearrange("p (k n) -> p k n", k=4)[:, :, 256 * j:256 * j + 256]
            if kind == "k":
                return r[:, 1024:1024 + P]
            if kind == "v":
                return r[:, 0:512]
            return r[:, 1024 * j:1024 * j + 1024]

        def split_view(w, kind, slot):
            s = w[:, slot, :]
            if kind == "cols":
                return s.rearrange("p (k n) -> p k n", k=KD)
            if kind == "a":
                return s[:, 0:2 * CA].rearrange("p (k n) -> p k n", k=2)
            if kind == "wo":
                return s.rearrange("p (k n) -> p k n", k=4)
            if kind == "k":
                return s[:, 0:P]
            if kind == "v":
                return s[:, 0:512]
            return s

        def q_views(w, slot):
            src = raw[:, 0, 0:2 * QK].rearrange("p (k n) -> p k n", k=2)
            dst = w[:, slot, 0:2 * P].rearrange("p (k n) -> p k n", k=2)
            halves = src[:, :, NOPE:QK].rearrange("p k (b n) -> p k b n", b=2)
            return [(dst[:, :, 0:QK], src),
                    (dst[:, :, QK:QK + HALF], halves[:, :, 1, :]),
                    (dst[:, :, QK + HALF:P], halves[:, :, 0, :])]

        def kind_of(t):
            if t < T_A or T_Y <= t < T_V:
                return "cols"
            if t < T_G0:
                return "a"
            if t == T_V:
                return "v"
            if t < T_HEAD:
                return "plain"
            if t < T_R:
                return ("q", "k", "cols", "cols")[(t - T_HEAD) % 4]
            if t < T_OUT:
                return "wo"
            if t < T_FFN:
                return "plain"
            return "cols" if t < T_DN else "plain"

        def tiles_in(t):
            return 2 if t == T_G0 else 1

        def split_hi(act, t0, dt=0):
            kind = kind_of(t0)
            if t0 % 2 == 0:
                act.wait_ge(raw_in[t0 // 2 % 2], dt * (PAIR_INC // 4) + PAIR_INC * (t0 // 4 + 1))
            if t0 >= 4:
                act.wait_ge(w_used, dt + t0 - 3)
            if kind == "q":
                for dst, src in q_views(w_hi, t0 % 4):
                    last = nc.scalar.activation(dst, src, ACT.Copy)
            else:
                last = nc.scalar.activation(split_view(w_hi, kind, t0 % 4), raw_view(kind, t0 // 2 % 2, t0 % 2), ACT.Copy)
            last.then_inc(w_half, tiles_in(t0))

        def split_lo(dve, t0, dt=0):
            kind = kind_of(t0)
            dve.wait_ge(w_half, dt + t0 + tiles_in(t0))
            if kind == "q":
                for (dst, src), (hi, _) in zip(q_views(w_lo, t0 % 4), q_views(w_hi, t0 % 4)):
                    last = nc.vector.tensor_tensor(dst, src, hi.bitcast(F32), ALU.subtract)
            else:
                last = nc.vector.tensor_tensor(split_view(w_lo, kind, t0 % 4), raw_view(kind, t0 // 2 % 2, t0 % 2),
                                               split_view(w_hi, kind, t0 % 4).bitcast(F32), ALU.subtract)
            last.then_inc(w_ready, tiles_in(t0))

        def tile_used(eng, t):
            eng.wait_ge(w_used, t + 1)

        def a_done_wait(eng, t):
            if t < NT - 1:
                eng.wait_ge(a_done, t + 1)
            else:
                tile_used(eng, T_A + 3)

        def gates_done(eng, d, part, n):
            if part and n == NB - 1:
                eng.wait_ge(w_used, (T_G1 if d else T_G0 + 1) + 1)
            else:
                eng.wait_ge(g_done, (2 * NB - 1) * d + NB * part + n + 1)

        def gate_bank(d, part, n):
            return (4 if d != part else 0) + n

        def v_done_wait(eng, t):
            if t < NT - 1:
                eng.wait_ge(v_done, t + 1)
            else:
                tile_used(eng, T_V)

        def branch_done(eng, first, branch, m):
            if m % 2 == 0:
                eng.wait_ge(first, m // 2 + 1)
            else:
                tile_used(eng, T_R + 4 * (m // 4) + 2 * branch + m % 4 // 2)

        def w_out_done(eng, c, t):
            if t < NT - 1:
                eng.wait_ge(wo_done, (NT - 1) * c + t + 1)
            else:
                tile_used(eng, T_OUT + 4 * c + 3)

        def product(dst, l_hi, l_lo, r_hi, r_lo, start, stop):
            nc.tensor.matmul(dst, l_lo, r_hi, start=start, stop=False)
            nc.tensor.matmul(dst, l_hi, r_lo, start=False, stop=False)
            return nc.tensor.matmul(dst, l_hi, r_hi, start=False, stop=stop)

        @block.sync
        def _(sync):
            def load(p0, dp, dst, src, inc=PAIR_INC):
                if p0 >= 2:
                    sync.wait_ge(w_ready, dp * 2 + 2 * p0 - 2)
                sync.dma_start(dst, src).then_inc(raw_in[p0 % 2], inc)

            def slot(p0):
                return raw[:, p0 % 2, :]

            def k_major(p0, k):
                return slot(p0).rearrange("p (k n) -> p k n", k=k)

            def load_x(t):
                sync.dma_start(xt[:, t, :], x_v[:, t, :]).then_inc(x_in[t], 16)

            def load_lru_x(p):
                load(p, 0, k_major(p, KD), w_in_v[:, :, C_LX + 256 * p:C_LX + 256 * p + 256])
            load_x(0)
            load_x(1)
            load_lru_x(0)
            load_x(2)
            load_x(3)
            load_lru_x(1)

            def row_load(r, src):
                sync.dma_start(rows[r:r + src.shape[0], :], src).then_inc(prm_in, 16)
            row_load(ROW_CW, conv_w[0].rearrange("j (n p) -> (j n) p", p=P))
            row_load(ROW_CB, conv_b[0].rearrange("(n p) -> n p", p=P))
            row_load(ROW_LAM, lru_lambda[0].rearrange("r (n p) -> (r n) p", p=P))
            row_load(ROW_BR, b_rgate[0].rearrange("r n p -> (r n) p"))
            row_load(ROW_BI, b_igate[0].rearrange("r n p -> (r n) p"))
            row_load(ROW_GQ, q_a_norm_g[0].rearrange("(n p) -> n p", p=P))
            row_load(ROW_GKV, kv_a_norm_g[0].rearrange("(n p) -> n p", p=P))
            row_load(ROW_G2, norm2_g[0].rearrange("(n p) -> n p", p=P))
            for p in (2, 3):
                load(p, 0, slot(p)[:, 0:4 * CA].rearrange("p (k n) -> p k n", k=4),
                     w_in_v[:, 4 * (p - 2):4 * (p - 2) + 4, 0:CA])

            sync.dma_start(tab_k[:, :, :, :], rope_k).then_inc(tab_in, 16)
            sync.dma_start(tab_q[:, :], rope_q).then_inc(tab_in, 16)

            def load_lru_gates(p, d, col, inc):
                for part, src in ((0, w_r_v), (1, w_i_v)):
                    load(p, 0, slot(p)[:, col + 512 * part:col + 512 * part + 512].rearrange("p (n d) -> p n d", n=NB),
                         src[:, d, :, :], inc=inc if part else 16)
            load_lru_gates(4, 0, 0, 32)
            for p in (5, 6):
                load(p, 0, k_major(p, KD), w_in_v[:, :, C_LY + 256 * (p - 5):C_LY + 256 * (p - 5) + 256])
            load_lru_gates(7, 1, 1024, 16)
            load(7, 0, slot(7)[:, 0:512].rearrange("p (h c) -> p h c", h=HEADS), w_val_v[:, :, 1, :], inc=16)
            p_head = T_HEAD // 2
            with sync.Fori(0, HEADS) as h:
                load(p_head, h * 2, slot(p_head)[:, 0:2 * QK].rearrange("p (k n) -> p k n", k=2),
                     w_qb_v[:, :, bass.ds(h * QK, QK)], inc=32)
                sync.dma_start(slot(p_head)[:, 1024:1024 + P], w_kvb_v[:, bass.ds(h * (NOPE + VD), NOPE + VD)]).then_inc(
                    raw_in[p_head % 2], 16)
                load(p_head + 1, h * 2, k_major(p_head + 1, KD), w_in_v[:, :, bass.ds(h * 256 + C_G, 256)])
            for n, src in enumerate((w_ol_v, w_oa_v, w_ol_v, w_oa_v)):
                load(T_R // 2 + n, 0, k_major(T_R // 2 + n, 4), src[:, :, 512 * (n // 2):512 * (n // 2) + 512])
            sync.wait_ge(rec_full, NB)
            sync.dma_start(xt[:, :, :], x_v).then_inc(x_back, 16)
            sync.dma_start(fin_g[:, :], final_g.rearrange("(a n) -> a n", a=1).to_broadcast([P, D])).then_inc(fin_in, 16)
            for n in range(4):
                load(T_OUT // 2 + n, 0, k_major(T_OUT // 2 + n, 4),
                     w_out_v[:, 4 * (n % 2):4 * (n % 2) + 4, 512 * (n // 2):512 * (n // 2) + 512])
            p_ffn = T_FFN // 2
            with sync.Fori(0, FT // 2) as i:
                load(p_ffn, i * 2, k_major(p_ffn, KD), w_fg_v[:, :, bass.ds(i * 256, 256)])
                load(p_ffn + 1, i * 2, k_major(p_ffn + 1, KD), w_fu_v[:, :, bass.ds(i * 256, 256)])
            p_dn = T_DN // 2
            with sync.Fori(0, FT // 4) as i:
                for j in range(2):
                    load(p_dn + j, i * 2, k_major(p_dn + j, 2), w_fd_v[:, bass.ds(i * 4 + 2 * j, 2), :])
            load(p_dn + FT // 2 - 1, 0, k_major(p_dn + FT // 2 - 1, 2), w_fd_v[:, FT - 2:FT, :])
            for t in range(NT):
                for c in range(2):
                    col = slice(512 * c, 512 * c + 512)
                    sync.wait_ge(fin_right if c else fin_left, t + 1)
                    sync.dma_start(out_v[:, t, col], xt[:, t, col]).then_inc(stored, 16)
            sync.wait_ge(stored, 16 * 2 * NT)

        @block.gpsimd
        def _(pool):
            nc.gpsimd.memset(ident[:, :], 0.0).then_inc(s_ident, 1)
            pool.wait_ge(s_ident, 1)
            nc.gpsimd.affine_select(out=ident[:, :], in_=ident[:, :], compare_op=ALU.not_equal, fill=1.0,
                                    base=0, pattern=[[-1, P]], channel_multiplier=1).then_inc(s_ident, 1)
            nc.gpsimd.memset(xp[:, :, 0:LEFT], 0.0)
            nc.gpsimd.memset(xp[:, :, LEFT + SEQ:], 0.0).then_inc(s_pad, 1)

            vs = f_hi[:, FV, :].rearrange("p (t c) -> p t c", t=NT)
            pool.wait_ge(v_ready, NT)
            pool.wait_ge(sig_ready, 16)

            def head_values(h):
                nc.gpsimd.tensor_copy(vs[:, :, 0:VD], val[:, :, bass.ds(h * VD, VD)]).then_inc(vs_half, 1)

            head_values(0)
            for n in range(NB):
                nc.gpsimd.tensor_tensor(lru_i[1][:, n, :], lru_i[1][:, n, :], xc[:, n, ::-1], ALU.mult).then_inc(ixc_ready, 1)
            for n in range(NB):
                nc.gpsimd.tensor_tensor(lru_i[0][:, n, :], lru_i[0][:, n, :], xc[:, n, :], ALU.mult).then_inc(ixc_ready, 1)
            def decayed_input(h, d, n):
                pool.wait_ge(ixc_ready, 2 * NB)
                pool.wait_ge(mult_ready, h + 1)
                nc.gpsimd.tensor_tensor(lru_i[d][:, n, :], lru_i[d][:, n, :], lru_m[:, :], ALU.mult).then_inc(u_ready, 1)

            decayed_input(0, 1, 0)
            with pool.Fori(1, NB) as h:
                pool.wait_ge(pv_done, h * NT)
                head_values(h)
                decayed_input(h, 1, h)
            for n in range(NB):
                pool.wait_ge(scan_done, n + 2)
                nc.gpsimd.tensor_copy(lru_h[:, n, :], lru_r[1][:, n, ::-1]).then_inc(turned, 1)
            with pool.Fori(0, NB - 1) as n:
                pool.wait_ge(pv_done, n * NT + NB * NT)
                head_values(n + NB)
                decayed_input(n + NB, 0, n)
                pool.wait_ge(scan_done, n + NB + 2)
                nc.gpsimd.tensor_tensor(lru_r[0][:, n, :], lru_r[0][:, n, :], lru_h[:, n, :], ALU.add).then_inc(hsum_ready, 1)
                pool.wait_ge(hsum_ready, n + 1)
                nc.gpsimd.tensor_tensor(lru_h[:, n, :], lru_r[0][:, n, :], lru_y[:, n, :], ALU.mult).then_inc(rec_full, 1)
            pool.wait_ge(pv_done, (HEADS - 1) * NT)
            head_values(HEADS - 1)
            decayed_input(HEADS - 1, 0, NB - 1)

            pool.wait_ge(fin_in, 16)
            for t in range(NT):
                for c in range(2):
                    col = slice(512 * c, 512 * c + 512)
                    pool.wait_ge(y2_ready, 2 * t + c + 1)
                    nc.gpsimd.tensor_tensor(yg[:, 2 * t + c, :], xt[:, t, col], fin_g[:, col], ALU.mult).then_inc(yg_ready, 1)

        @block.scalar
        def _(act):
            act.dma_start(rows[ROW_G1:ROW_G1 + KD, :], norm1_g[0].rearrange("(n p) -> n p", p=P)).then_inc(g1_in, 16)
            act.wait_ge(s_ident, 2)
            nc.scalar.activation(nwt[:, 7:8], ident[:, 0:1], ACT.Sqrt)

            sums = [0]

            def square_sum(src, r, t, junk, scale=1.0):
                if sums[0] > 1:
                    act.wait_ge(ssq_ready, sums[0] - 1)
                sums[0] += 1
                nc.scalar.activation(junk, src, ACT.Square, scale=scale, accum_out=ssq[:, r, t:t + 1]).then_inc(ssq_ready, 1)

            def root(r, t, n, count):
                act.wait_ge(rms_ready, count)
                nc.scalar.activation(rstd[:, r, t:t + n], rms[:, r, t:t + n], ACT.Sqrt).then_inc(rstd_ready, 1)

            def norm_hi(row, base, half, n0, count):
                tok = slice(256 * half, 256 * half + 256)
                for b in range(KD // 2):
                    act.wait_ge(xT_done, n0 + 4 * half + b + 1)
                    for j in range(2):
                        d = 2 * b + j
                        nc.scalar.activation(hT_hi[:, d, tok], ps[:, base + b, 256 * j:256 * j + 256], ACT.Copy,
                                             scale=prm[:, row + d:row + d + 1]).then_inc(count, 1)

            for half in range(2):
                for t in (2 * half, 2 * half + 1):
                    act.wait_ge(x_in[t], 16)
                    square_sum(xt[:, t, :], 0, t, sq_junk[:, t % 2, :])
                root(0, 2 * half, 2, half + 1)
                split_hi(act, 2 * half)
                split_hi(act, 2 * half + 1)
                if not half:
                    act.wait_ge(prm_ready, 1)
                norm_hi(ROW_G1, 4, half, 0, h_half)
            act.wait_ge(lam_neg, 1)
            nc.scalar.activation(sp[:, 1, :], sp[:, 0, :], ACT.Exp).then_inc(lam_exp, 1)
            act.wait_ge(s_pad, 1)
            for n in range(NB):
                tile_used(act, T_X + n)
                nc.scalar.activation(xp[:, n, LEFT:LEFT + SEQ], ps[:, n, :], ACT.Copy).then_inc(xp_ready, 1)
                split_hi(act, T_A + n)
            for n in range(NB):
                act.wait_ge(xc_full, n + 1)
                nc.scalar.activation(f_hi[:, FXC + n, :], xc[:, n, :], ACT.Copy).then_inc(xc_half, 1)
                if n == 0:
                    split_hi(act, T_G0)
                if n in (2, 3):
                    split_hi(act, T_Y + n - 2)

            def gate_sigmoids(d, part, blocks=range(NB)):
                for n in blocks:
                    gates_done(act, d, part, n)
                    b = gate_bank(d, part, n)
                    col = (ROW_BI if part else ROW_BR) + NB * d + n
                    src = ps[:, b, ::-1] if d else ps[:, b, :]
                    nc.scalar.activation((lru_i if part else lru_r)[d][:, n, :], src, ACT.Sigmoid,
                                         bias=prm[:, col:col + 1]).then_inc(sig_ready, 1)

            gate_sigmoids(0, 0)
            for t in range(NT):
                act.wait_ge(pa_ready, t + 1)
                square_sum(pa[:, t, 0:QL], 1, t, sq_junk[:, 0, 0:QL])
                square_sum(pa[:, t, QL:QL + KVL], 1, NT + t, sq_junk[:, 1, 0:KVL])
            root(1, 0, 2 * NT, 3)
            gate_sigmoids(0, 1)
            for t in (T_Y + 2, T_Y + 3, T_V):
                split_hi(act, t)
            act.wait_ge(aT_done, 1)
            for m in range(3):
                act.wait_ge(aT_done, m + 1)
                nc.scalar.activation(f_hi[:, FQA + m, :], ps[:, 4 + m, :], ACT.Copy,
                                     scale=prm[:, ROW_GQ + m:ROW_GQ + m + 1]).then_inc(aT_half, 1)
            act.wait_ge(aT_done, 4)
            nc.scalar.activation(f_hi[NOPE:QK, FK, :], ps[NOPE:QK, 7, :], ACT.Copy).then_inc(aT_half, 1)
            split_hi(act, T_G1)
            for m in range(NB):
                tile_used(act, T_Y + m)
                nc.scalar.activation(lru_y[:, m, :], ps[:, m, :], ACT.Gelu_apprx_tanh).then_inc(y_ready, 1)
                if m < 2:
                    split_hi(act, T_HEAD + m)
            gate_sigmoids(1, 0)
            gate_sigmoids(1, 1, (0, 1))
            split_hi(act, T_HEAD + 2)
            gate_sigmoids(1, 1, (2, 3))

            def decay_block(d, n):
                col, r = n + NB * d, lru_r[d][:, n, :]
                nc.scalar.activation(lru_a, r, ACT.Exp, scale=decay[:, 1, bass.ds(col, 1)])
                nc.scalar.activation(lru_t, r, ACT.Tanh, scale=decay[:, 0, bass.ds(col, 1)])
                nc.scalar.activation(r, r, ACT.Exp, scale=decay[:, 2, bass.ds(col, 1)]).then_inc(exp3_ready, 1)

            def k_hi(h):
                tile_used(act, h * 4 + T_HEAD + 1)
                nc.scalar.activation(f_hi[0:NOPE, FK, :], ps[0:NOPE, 1, :], ACT.Copy).then_inc(k_half, 1)

            def q_hi(h):
                act.wait_ge(q_full, h + 1)
                nc.scalar.activation(f_hi[0:QK, FQ, :], q_f[0:QK, :], ACT.Copy).then_inc(q_half, 1)

            def rec_hi(n):
                act.wait_ge(rec_full, n + 1)
                nc.scalar.activation(f_hi[:, FREC + n, :], lru_h[:, n, :], ACT.Copy).then_inc(rec_half, 1)

            def o_hi(n):
                nc.scalar.activation(f_hi[:, FO + n, :], o_t[:, n, :], ACT.Copy).then_inc(ot_half, 1)

            def head(h, h0, d, last=False):
                t0, dt = T_HEAD + 4 * h0 + 4, (h - h0) * 4
                for t in range(NT):
                    act.wait_ge(nb_ready, h * 2 + t // 2 + 1)
                    nc.scalar.activation(prob[:, t, :], ps[:, 4 + t, :], ACT.Exp, bias=nbias[:, t:t + 1], scale=SCALE,
                                         accum_out=psum_p[:, t:t + 1]).then_inc(e_ready, 1)
                act.wait_ge(scan_done, h + 1)
                decay_block(d, h - NB * (1 - d))
                tile_used(act, h * 4 + T_HEAD + 2)
                if not d:
                    act.wait_ge(turned, NB)
                nc.scalar.activation(store[:, h * 2, :], ps[:, 2, :], ACT.Tanh, scale=0.5).then_inc(gl_ready, 1)
                split_hi(act, t0, dt)
                if not last:
                    split_hi(act, t0 + 1, dt)
                for kt in range(NT):
                    act.wait_ge(t_done, h * 4 + kt + 1)
                    if kt >= 2:
                        act.wait_ge(pv_done, h * 4 + kt - 1)
                    nc.scalar.activation(f_hi[:, FPT + kt % 2, :], ps[:, 4 + kt, :], ACT.Copy).then_inc(pt_half, 1)
                    if kt == 1:
                        if not last:
                            split_hi(act, t0 + 2, dt)
                        act.wait_ge(m2_ready, h + 1)
                        nc.scalar.activation(lru_m[:, :], lru_m[:, :], ACT.Sqrt).then_inc(mult_ready, 1)
                    if last and kt == 1:
                        rec_hi(0)
                        rec_hi(1)
                    if last and kt == 3:
                        rec_hi(2)
                if not last:
                    k_hi(h + 1)
                else:
                    split_hi(act, t0 + 1)
                act.wait_ge(pv_done, h * 4 + 4)
                nc.scalar.activation(o_half[0:VD, :], ps[VD:P, 4, :], ACT.Copy).then_inc(oc_ready, 1)
                if not last:
                    q_hi(h + 1)
                    split_hi(act, t0 + 3, dt)
                tile_used(act, h * 4 + T_HEAD + 3)
                nc.scalar.activation(store[:, h * 2 + 1, :], ps[:, 3, :], ACT.Tanh, scale=0.5).then_inc(gl_ready, 1)

            act.wait_ge(decay_ready, 3)
            act.wait_ge(sig_ready, 16)
            k_hi(0)
            q_hi(0)
            split_hi(act, T_HEAD + 3)
            with act.Fori(0, NB) as h:
                head(h, 0, 1)
            with act.Fori(NB, HEADS - 1) as h:
                head(h, 0, 0)
            head(HEADS - 1, HEADS - 1, 0, last=True)

            rec_hi(NB - 1)
            split_hi(act, T_R + 2)
            for n in range(NB - 1):
                o_hi(n)
            split_hi(act, T_R + 3)
            act.wait_ge(o_ready, HEADS + 1)
            o_hi(NB - 1)
            for n in range(4):
                split_hi(act, T_R + 4 + n)
            for m in range(KD):
                act.wait_ge(mg_full, m + 1)
                nc.scalar.activation(hT_hi[:, m, :], store[:, m, :], ACT.Copy, scale=0.5).then_inc(mg_half, 1)
                for t in {3: (0, 1), 4: (2,), 6: (3,)}.get(m, ()):
                    split_hi(act, T_OUT + t)

            for t in range(4):
                split_hi(act, T_OUT + 4 + t)
            def norm_square(t):
                act.wait_ge(x2_ready, NT + t + 1)
                square_sum(xt[:, t, :], 2, t, sq_junk[:, t % 2, :])

            for t in range(2):
                norm_square(t)
                root(2, t, 1, 4 + t)
            norm_square(2)
            root(2, 2, 1, 6)
            split_hi(act, T_FFN)
            split_hi(act, T_FFN + 1)
            norm_hi(ROW_G2, 0, 0, KD, h2_half)
            norm_square(3)
            root(2, 3, 1, 7)
            for t in (2, 3):
                split_hi(act, T_FFN + t)
            norm_hi(ROW_G2, 0, 1, KD, h2_half)

            act.sem_inc(silu_ready, 2)

            def act_hi(n0, dn=0):
                act.wait_ge(act_ready, dn + n0 + 3)
                nc.scalar.activation(f_hi[:, FACT + n0 % 4, :], store[:, dn + n0, :], ACT.Copy).then_inc(act_half, 1)

            def ffn(i, i0):
                for j in range(2):
                    tile_used(act, i * 4 + T_FFN + j)
                    act.wait_ge(act_ready, i * 2 + j + 1)
                    nc.scalar.activation(silu[:, j, :], ps[:, 4 + j, :], ACT.Silu).then_inc(silu_ready, 1)
                    split_hi(act, T_FFN + 4 * i0 + 4 + j, (i - i0) * 4)
                    if i0:
                        act_hi(j)
                for j in range(2, 4):
                    split_hi(act, T_FFN + 4 * i0 + 4 + j, (i - i0) * 4)
                    if i0:
                        act_hi(j)

            with act.Fori(0, FT // 2 - 1) as i:
                ffn(i, 0)
            ffn(FT // 2 - 1, FT // 2 - 1)

            with act.Fori(0, 4) as i:
                for j in range(4):
                    split_hi(act, T_DN + 4 + j, i * 4)
                    act_hi(4 + j, i * 4)
            for n in (FT - 2, FT - 1):
                split_hi(act, T_DN + n)
                act_hi(n)

            def last_square(t, c):
                act.wait_ge(y2_ready, 2 * t + c + 1)
                square_sum(xt[:, t, 512 * c:512 * c + 512], 3, 2 * t + c, sq_junk[:, c, 0:512], scale=float(D) ** -0.5)

            def last_scale(t):
                act.wait_ge(scale_ready, t + 1)
                act.wait_ge(yg_ready, 2 * t + 1)
                nc.scalar.activation(xt[:, t, 0:512], yg[:, 2 * t, :], ACT.Copy, scale=rstd[:, 3, t:t + 1]).then_inc(fin_left, 1)

            for t in range(NT):
                last_square(t, 0)
                last_square(t, 1)
                if t:
                    last_scale(t - 1)
                root(3, t, 1, NT + 4 + t)
            last_scale(NT - 1)

        @block.vector
        def _(dve):
            steps = [0]

            def link(ins):
                steps[0] += 1
                ins.then_inc(dve_step, 1)
                dve.wait_ge(dve_step, steps[0])

            def mean(r, t, n, width, ssq_count):
                dve.wait_ge(ssq_ready, ssq_count)
                link(nc.vector.tensor_scalar(mse[:, r, t:t + n], ssq[:, r, t:t + n], 1.0 / width, EPS, ALU.mult, ALU.add))

            def inverse(r, t, n):
                nc.vector.reciprocal(rms[:, r, t:t + n], mse[:, r, t:t + n]).then_inc(rms_ready, 1)

            def refine(r, t, n, rstd_count, done=None):
                y, m, z = rstd[:, r, t:t + n], mse[:, r, t:t + n], nwt[:, 0:n]
                dve.wait_ge(rstd_ready, rstd_count)
                if n == 1:
                    link(nc.vector.scalar_tensor_tensor(z, y, m, y, ALU.mult, ALU.mult))
                else:
                    link(nc.vector.tensor_tensor(z, y, y, ALU.mult))
                    link(nc.vector.tensor_tensor(z, z, m, ALU.mult))
                link(nc.vector.tensor_scalar(z, z, -0.5, 1.5, ALU.mult, ALU.add))
                ins = nc.vector.tensor_tensor(y, y, z, ALU.mult)
                if done is None:
                    link(ins)
                else:
                    ins.then_inc(done, 1)

            def norm_begin(r, t, ssq_count):
                mean(r, t, 1, D, ssq_count)
                inverse(r, t, 1)

            def norm_end(r, t, dst, rstd_count):
                refine(r, t, 1, rstd_count)
                nc.vector.tensor_scalar(dst, xt[:, t, :], rstd[:, r, t:t + 1], None, ALU.mult).then_inc(xn_ready, 1)

            def norm_lo(row, base, half, count, done):
                tok = slice(256 * half, 256 * half + 256)
                for b in range(KD // 2):
                    dve.wait_ge(count, KD * half + 2 * b + 2)
                    for j in range(2):
                        d = 2 * b + j
                        nc.vector.scalar_tensor_tensor(
                            hT_lo[:, d, tok], ps[:, base + b, 256 * j:256 * j + 256], prm[:, row + d:row + d + 1],
                            hT_hi[:, d, tok].bitcast(F32), ALU.mult, ALU.subtract).then_inc(done, 1)

            dve.wait_ge(prm_t, 1)
            nc.vector.tensor_copy(prm[:, ROW_G1:ROW_G1 + KD], ps[:, 7, 0:KD]).then_inc(prm_ready, 1)
            for half in range(2):
                mean(0, 2 * half, 2, D, 2 * half + 2)
                inverse(0, 2 * half, 2)
                refine(0, 2 * half, 2, half + 1)
                for t in (2 * half, 2 * half + 1):
                    nc.vector.tensor_scalar(xt[:, t, :], xt[:, t, :], rstd[:, 0, t:t + 1], None, ALU.mult).then_inc(xn_ready, 1)
                split_lo(dve, 2 * half)
                split_lo(dve, 2 * half + 1)
                norm_lo(ROW_G1, 4, half, h_half, h_ready)
            dve.wait_ge(prm_t, 2)
            nc.vector.tensor_copy(prm[:, KD:N_ROWS], ps[:, 7, KD:N_ROWS]).then_inc(prm_ready, 1)
            dve.wait_ge(prm_ready, 2)
            lam = prm[:, ROW_LAM:ROW_LAM + 8]
            nc.vector.scalar_tensor_tensor(sp[:, 0, :], lam, -1.0, lam, ALU.mult, ALU.min).then_inc(lam_neg, 1)

            for n in range(NB):
                dve.wait_ge(xp_ready, n + 1)
                tap = [prm[:, ROW_CW + NB * j + n:ROW_CW + NB * j + n + 1] for j in range(TAPS)]
                link(nc.vector.tensor_scalar(xc[:, n, :], xp[:, n, 0:SEQ], tap[0], prm[:, ROW_CB + n:ROW_CB + n + 1],
                                             ALU.mult, ALU.add))
                for j in range(1, TAPS):
                    ins = nc.vector.scalar_tensor_tensor(xc[:, n, :], xp[:, n, j:j + SEQ], tap[j], xc[:, n, :],
                                                         ALU.mult, ALU.add)
                    if j < TAPS - 1:
                        link(ins)
                    else:
                        ins.then_inc(xc_full, 1)
                split_lo(dve, T_A + n)
            for n in range(NB):
                dve.wait_ge(xc_half, n + 1)
                nc.vector.tensor_tensor(f_lo[:, FXC + n, :], xc[:, n, :], f_hi[:, FXC + n, :].bitcast(F32),
                                        ALU.subtract).then_inc(xc_ready, 1)
                if n == 0:
                    split_lo(dve, T_G0)
                if n in (2, 3):
                    split_lo(dve, T_Y + n - 2)

            for t in range(NT):
                a_done_wait(dve, t)
                nc.vector.tensor_copy(pa[:, t, :], ps[:, 4 + t, 0:CA]).then_inc(pa_ready, 1)

            dve.wait_ge(lam_exp, 1)
            e, s, s2, q, r = (sp[:, k, :] for k in (1, 2, 3, 4, 5))
            link(nc.vector.tensor_scalar(r, e, 2.0, None, ALU.add))
            link(nc.vector.reciprocal(r, r))
            link(nc.vector.tensor_tensor(s, e, r, ALU.mult))
            link(nc.vector.tensor_tensor(s2, s, s, ALU.mult))
            link(nc.vector.tensor_scalar(q, s2, 1.0 / 17, None, ALU.mult))
            for k in (15, 13, 11, 9, 7, 5, 3):
                link(nc.vector.scalar_tensor_tensor(q, q, 1.0 / k, s2, ALU.add, ALU.mult))
            link(nc.vector.scalar_tensor_tensor(q, q, 1.0, s, ALU.add, ALU.mult))
            link(nc.vector.tensor_scalar(r, lam, -1.0, 0.0, ALU.mult, ALU.max))
            link(nc.vector.scalar_tensor_tensor(q, q, 2.0, r, ALU.mult, ALU.add))
            for k, f in enumerate((LRU_C, -LRU_C, -2 * LRU_C)):
                nc.vector.tensor_scalar(decay[:, k, :], q, f, None, ALU.mult).then_inc(decay_ready, 1)

            mean(1, 0, NT, QL, 3 * NT)
            mean(1, NT, NT, KVL, 3 * NT)
            inverse(1, 0, 2 * NT)
            dve.wait_ge(tab_in, 32)
            dve.wait_ge(pa_ready, NT)
            k1, k2 = pa[:, :, QL + KVL:QL + KVL + HALF], pa[:, :, QL + KVL + HALF:CA]
            cos, sin = tab_k[:, :, 0, :], tab_k[:, :, 1, :]
            for dst, a, b in ((0, k1, cos), (1, k2, sin), (2, k2, cos)):
                nc.vector.tensor_tensor(ksc[:, dst, :, :], a, b, ALU.mult)
            link(nc.vector.tensor_tensor(ksc[:, 3, :, :], k1, sin, ALU.mult))
            nc.vector.tensor_tensor(k1, ksc[:, 0, :, :], ksc[:, 1, :, :], ALU.subtract)
            nc.vector.tensor_tensor(k2, ksc[:, 2, :, :], ksc[:, 3, :, :], ALU.add)
            refine(1, 0, 2 * NT, 3)
            for t in range(NT):
                nc.vector.tensor_scalar(pa[:, t, 0:QL], pa[:, t, 0:QL], rstd[:, 1, t:t + 1], None, ALU.mult)
                nc.vector.tensor_scalar(pa[:, t, QL:QL + KVL], pa[:, t, QL:QL + KVL], rstd[:, 1, NT + t:NT + t + 1],
                                        None, ALU.mult).then_inc(pa_norm, 1)
            for t in (T_Y + 2, T_Y + 3, T_V):
                split_lo(dve, t)
            for m in range(3):
                dve.wait_ge(aT_half, m + 1)
                nc.vector.scalar_tensor_tensor(f_lo[:, FQA + m, :], ps[:, 4 + m, :], prm[:, ROW_GQ + m:ROW_GQ + m + 1],
                                               f_hi[:, FQA + m, :].bitcast(F32), ALU.mult, ALU.subtract).then_inc(aT_ready, 1)
            dve.wait_ge(aT_half, 4)
            nc.vector.tensor_tensor(f_lo[NOPE:QK, FK, :], ps[NOPE:QK, 7, :], f_hi[NOPE:QK, FK, :].bitcast(F32),
                                    ALU.subtract).then_inc(aT_ready, 1)
            split_lo(dve, T_G1)
            split_lo(dve, T_HEAD)
            split_lo(dve, T_HEAD + 1)
            for t in range(NT):
                v_done_wait(dve, t)
                nc.vector.tensor_copy(val[:, t, :], ps[:, 4 + t, :]).then_inc(v_ready, 1)
            dve.wait_ge(y_ready, NB)
            nc.vector.sem_inc(gl_ready, 2)
            nc.vector.sem_inc(o_ready, 1)
            nc.vector.sem_inc(scan_done, 1)
            split_lo(dve, T_HEAD + 2)

            vs = f_hi[:, FV, :].rearrange("p (t c) -> p t c", t=NT)

            def qk_lo(h):
                tile_used(dve, h * 4 + T_HEAD)
                nc.vector.tensor_tensor(q_s[NOPE:QK, :], ps[QK:P, 0, :], tab_q[QK:P, :], ALU.mult)
                nc.vector.tensor_tensor(q_f[0:QK, :], ps[0:QK, 0, :], tab_q[0:QK, :], ALU.mult).then_inc(q_prod, 1)
                dve.wait_ge(q_prod, h + 1)
                nc.vector.tensor_tensor(q_f[NOPE:QK, :], q_f[NOPE:QK, :], q_s[NOPE:QK, :], ALU.add).then_inc(q_full, 1)
                dve.wait_ge(k_half, h + 1)
                nc.vector.tensor_tensor(f_lo[0:NOPE, FK, :], ps[0:NOPE, 1, :], f_hi[0:NOPE, FK, :].bitcast(F32),
                                        ALU.subtract).then_inc(k_ready, 1)
                dve.wait_ge(q_half, h + 1)
                nc.vector.tensor_tensor(f_lo[0:QK, FQ, :], q_f[0:QK, :], f_hi[0:QK, FQ, :].bitcast(F32),
                                        ALU.subtract).then_inc(q_ready, 1)

            def rec_lo(n):
                dve.wait_ge(rec_half, n + 1)
                nc.vector.tensor_tensor(f_lo[:, FREC + n, :], lru_h[:, n, :], f_hi[:, FREC + n, :].bitcast(F32),
                                        ALU.subtract).then_inc(rec_ready, 1)

            def o_lo(n):
                dve.wait_ge(ot_half, n + 1)
                nc.vector.tensor_tensor(f_lo[:, FO + n, :], o_t[:, n, :], f_hi[:, FO + n, :].bitcast(F32),
                                        ALU.subtract).then_inc(ot_ready, 1)

            def head(h, h0, d, out_slice, last=False):
                t0, dt = T_HEAD + 4 * h0 + 4, (h - h0) * 4
                n = h - NB * (1 - d)
                r = lru_r[d][:, n, :]
                for c in range(2):
                    dve.wait_ge(sc_done, h * 4 + 2 * c + 2)
                    nc.vector.reduce_max(mx[:, 2 * c:2 * c + 2], ps[:, 4 + 2 * c:6 + 2 * c, :], AX_X).then_inc(max_ready, 1)
                    dve.wait_ge(max_ready, h * 2 + c + 1)
                    nc.vector.tensor_scalar(nbias[:, 2 * c:2 * c + 2], mx[:, 2 * c:2 * c + 2], -SCALE, None,
                                            ALU.mult).then_inc(nb_ready, 1)
                dve.wait_ge(vs_half, h + 1)
                nc.vector.tensor_tensor(vs[:, :, VD:P], val[:, :, bass.ds(h * VD, VD)], vs[:, :, 0:VD].bitcast(F32),
                                        ALU.subtract).then_inc(vs_ready, 1)
                for t in range(NT):
                    dve.wait_ge(e_ready, h * 4 + t + 1)
                    nc.vector.reciprocal(rsum[:, t:t + 1], psum_p[:, t:t + 1]).then_inc(rs_ready, 1)
                    dve.wait_ge(rs_ready, h * 4 + t + 1)
                    nc.vector.tensor_scalar(prob[:, t, :], prob[:, t, :], rsum[:, t:t + 1], None, ALU.mult).then_inc(p_ready, 1)
                dve.wait_ge(exp3_ready, h + 1)
                nc.vector.scalar_tensor_tensor(lru_m[:, :], r, 1.0, lru_t, ALU.add, ALU.mult).then_inc(m2_ready, 1)
                split_lo(dve, t0, dt)
                if not last:
                    split_lo(dve, t0 + 1, dt)
                for kt in range(NT):
                    dve.wait_ge(pt_half, h * 4 + kt + 1)
                    nc.vector.tensor_tensor(f_lo[:, FPT + kt % 2, :], ps[:, 4 + kt, :], f_hi[:, FPT + kt % 2, :].bitcast(F32),
                                            ALU.subtract).then_inc(pt_ready, 1)
                    if kt == 1 and not last:
                        split_lo(dve, t0 + 2, dt)
                    if last and kt == 1:
                        rec_lo(0)
                        rec_lo(1)
                    if last and kt == 3:
                        rec_lo(2)
                if not last:
                    qk_lo(h + 1)
                else:
                    split_lo(dve, t0 + 1)
                if d:
                    dve.wait_ge(ixc_ready, 2 * NB)
                dve.wait_ge(oc_ready, h + 1)
                nc.vector.tensor_tensor(out_slice, ps[0:VD, 4, :], o_half[0:VD, :], ALU.add).then_inc(o_ready, 1)
                if not last:
                    split_lo(dve, t0 + 3, dt)
                dve.wait_ge(u_ready, h + 1)
                nc.vector.tensor_tensor_scan(r, lru_a, lru_i[d][:, n, :], 0.0, ALU.mult, ALU.add).then_inc(scan_done, 1)

            qk_lo(0)
            split_lo(dve, T_HEAD + 3)
            with dve.Fori(0, NB // 2) as i:
                for j in range(2):
                    head(i * 2 + j, 0, 1, o_t[VD * j:VD * j + VD, i, :])
            for h in range(NB, HEADS):
                head(h, h, 0, o_t[VD * (h % 2):VD * (h % 2) + VD, h // 2, :], last=h == HEADS - 1)

            dve.wait_ge(scan_done, 2 * NB + 1)
            dve.wait_ge(turned, NB)
            link(nc.vector.tensor_tensor(lru_h[:, NB - 1, :], lru_h[:, NB - 1, :], lru_r[0][:, NB - 1, :], ALU.add))
            nc.vector.tensor_tensor(lru_h[:, NB - 1, :], lru_h[:, NB - 1, :], lru_y[:, NB - 1, :], ALU.mult).then_inc(rec_full, 1)
            rec_lo(NB - 1)
            split_lo(dve, T_R + 2)
            for n in range(NB - 1):
                o_lo(n)
            split_lo(dve, T_R + 3)
            o_lo(NB - 1)
            dve.wait_ge(gl_ready, 2 * HEADS + 2)
            for half in range(2):
                for m in range(4 * half, 4 * half + 4):
                    branch_done(dve, rl_done, 0, m)
                    nc.vector.scalar_tensor_tensor(store[:, KD + m, :], store[:, KD + m, :], 1.0, ps[:, m % 4, :],
                                                   ALU.add, ALU.mult).then_inc(rl_gated, 1)
                    if m % 2 == 0:
                        split_lo(dve, T_R + 4 * half + 4 + m % 4 // 2) if not half else split_lo(dve, T_OUT + m % 4 // 2)
                for m in range(4 * half, 4 * half + 4):
                    branch_done(dve, ra_done, 1, m)
                    nc.vector.scalar_tensor_tensor(store[:, m, :], store[:, m, :], 1.0, ps[:, 4 + m % 4, :],
                                                   ALU.add, ALU.mult).then_inc(ra_gated, 1)
                    dve.wait_ge(ra_gated, m + 1)
                    dve.wait_ge(rl_gated, m + 1)
                    nc.vector.tensor_tensor(store[:, m, :], store[:, m, :], store[:, KD + m, :], ALU.add).then_inc(mg_full, 1)
                    dve.wait_ge(mg_half, m + 1)
                    nc.vector.scalar_tensor_tensor(hT_lo[:, m, :], store[:, m, :], 0.5, hT_hi[:, m, :].bitcast(F32),
                                                   ALU.mult, ALU.subtract).then_inc(mg_ready, 1)
                    if m % 2 == 0:
                        split_lo(dve, T_R + 4 * half + 6 + m % 4 // 2) if not half else split_lo(dve, T_OUT + 2 + m % 4 // 2)
            for t in range(4):
                split_lo(dve, T_OUT + 4 + t)

            dve.wait_ge(x_back, 16)

            def residual_1(t, c):
                w_out_done(dve, c, t)
                part = xt[:, t, 512 * c:512 * c + 512]
                nc.vector.tensor_tensor(part, part, ps[:, 4 * c + t, :], ALU.add).then_inc(x2_ready, 1)

            for t in range(NT):
                residual_1(t, 0)
            for t in range(2):
                residual_1(t, 1)
                norm_begin(2, t, 3 * NT + t + 1)
                norm_end(2, t, xn[:, t, :], 4 + t)
            residual_1(2, 1)
            norm_begin(2, 2, 4 * NT - 1)
            norm_end(2, 2, xn[:, 2, :], 6)
            split_lo(dve, T_FFN)
            norm_lo(ROW_G2, 0, 0, h2_half, h2_ready)
            split_lo(dve, T_FFN + 1)
            residual_1(3, 1)
            norm_begin(2, 3, 4 * NT)
            norm_end(2, 3, xn[:, 3, :], 7)
            for t in (2, 3):
                split_lo(dve, T_FFN + t)
            norm_lo(ROW_G2, 0, 1, h2_half, h2_ready)

            nc.vector.sem_inc(act_ready, 2)

            def act_lo(n0, dn=0):
                dve.wait_ge(act_half, dn + n0 + 1)
                nc.vector.tensor_tensor(f_lo[:, FACT + n0 % 4, :], store[:, dn + n0, :],
                                        f_hi[:, FACT + n0 % 4, :].bitcast(F32), ALU.subtract).then_inc(act_split, 1)

            def ffn(i, i0):
                for j in range(2):
                    split_lo(dve, T_FFN + 4 * i0 + 4 + j, (i - i0) * 4)
                    if i0:
                        act_lo(j)
                for j in range(2):
                    dve.wait_ge(silu_ready, i * 2 + j + 3)
                    tile_used(dve, i * 4 + T_FFN + 2 + j)
                    nc.vector.tensor_tensor(store[:, i * 2 + j, :], silu[:, j, :], ps[:, 6 + j, :],
                                            ALU.mult).then_inc(act_ready, 1)
                    split_lo(dve, T_FFN + 4 * i0 + 6 + j, (i - i0) * 4)
                    if i0:
                        act_lo(2 + j)

            with dve.Fori(0, FT // 2 - 1) as i:
                ffn(i, 0)
            ffn(FT // 2 - 1, FT // 2 - 1)
            with dve.Fori(0, 4) as i:
                for j in range(4):
                    split_lo(dve, T_DN + 4 + j, i * 4)
                    act_lo(4 + j, i * 4)
            for n in (FT - 2, FT - 1):
                split_lo(dve, T_DN + n)
                act_lo(n)

            def residual(t, c):
                dve.wait_ge(dn_done, 2 * t + c + 1)
                part = xt[:, t, 512 * c:512 * c + 512]
                nc.vector.tensor_tensor(part, part, ps[:, 2 * t + c, :], ALU.add).then_inc(y2_ready, 1)

            def last_root(t):
                dve.wait_ge(ssq_ready, 4 * NT + 2 * t + 2)
                link(nc.vector.scalar_tensor_tensor(mse[:, 3, t:t + 1], ssq[:, 3, 2 * t:2 * t + 1], EPS,
                                                    ssq[:, 3, 2 * t + 1:2 * t + 2], ALU.add, ALU.add))
                inverse(3, t, 1)

            def last_scale(t):
                refine(3, t, 1, NT + 4 + t, done=scale_ready)
                dve.wait_ge(scale_ready, t + 1)
                dve.wait_ge(yg_ready, 2 * t + 2)
                nc.vector.tensor_scalar(xt[:, t, 512:D], yg[:, 2 * t + 1, :], rstd[:, 3, t:t + 1], None,
                                        ALU.mult).then_inc(fin_right, 1)

            for t in range(NT):
                residual(t, 0)
                residual(t, 1)
                if t:
                    last_scale(t - 1)
                last_root(t)
            last_scale(NT - 1)

        @block.tensor
        def _(pe):
            def cols_tile(t0, dt, bank, ks=range(KD)):
                wh = split_view(w_hi, "cols", t0 % 4)
                wl = split_view(w_lo, "cols", t0 % 4)
                if 0 in ks:
                    pe.wait_ge(w_ready, dt + t0 + 1)
                for k in ks:
                    last = product(ps[:, bank, :], wh[:, k, :], wl[:, k, :], hT_hi[:, k, :], hT_lo[:, k, :],
                                   k == 0, k == KD - 1)
                return last

            def used(ins, n=1):
                ins.then_inc(w_used, n)

            pe.wait_ge(s_ident, 2)
            pe.wait_ge(g1_in, 16)
            nc.tensor.transpose(ps[:, 7, 0:KD], rows[0:KD, :], ident[0:KD, 0:KD]).then_inc(prm_t, 1)

            def transpose_half(src, count, half, base):
                for j in range(2):
                    t = 2 * half + j
                    pe.wait_ge(xn_ready, count + t + 1)
                    for d in range(KD):
                        col = 256 * (d % 2) + P * j
                        ins = nc.tensor.transpose(ps[:, base + d // 2, col:col + P], src[:, t, P * d:P * d + P], ident[:, :])
                        if j and d % 2:
                            ins.then_inc(xT_done, 1)

            def half_tile(t0, bank, half, h_sem=None):
                tok = slice(256 * half, 256 * half + 256)
                wh, wl = split_view(w_hi, "cols", t0 % 4), split_view(w_lo, "cols", t0 % 4)
                pe.wait_ge(w_ready, t0 + 1)
                for k in range(KD):
                    if h_sem is not None:
                        pe.wait_ge(h_sem, KD * half + k + 1)
                    last = product(ps[:, bank, tok], wh[:, k, :], wl[:, k, :], hT_hi[:, k, tok], hT_lo[:, k, tok],
                                   k == 0, k == KD - 1)
                return last

            def norm_and_tiles(src, count, base, t0, bank, h_sem, bank_free=None):
                for j in range(4):
                    if bank_free is not None:
                        bank_free(j)
                    half_tile(t0 + j, bank + j, 0, h_sem if not j else None)
                    if j == 1:
                        transpose_half(src, count, 1, base)
                for j in range(4):
                    used(half_tile(t0 + j, bank + j, 1, h_sem if not j else None))
                    if j == 0 and bank_free is None:
                        pe.wait_ge(prm_in, 16 * 8)
                        nc.tensor.transpose(ps[:, 7, 0:N_ROWS], rows[0:N_ROWS, :],
                                            ident[0:N_ROWS, 0:N_ROWS]).then_inc(prm_t, 1)

            pe.wait_ge(prm_ready, 1)
            transpose_half(xt, 0, 0, 4)
            norm_and_tiles(xt, 0, 4, T_X, 0, h_ready)
            pe.wait_ge(prm_ready, 2)
            for n in range(4):
                t0 = T_A + n
                pe.wait_ge(w_ready, t0 + 1)
                wh, wl = split_view(w_hi, "a", t0 % 4), split_view(w_lo, "a", t0 % 4)
                for kk in range(2):
                    k = 2 * n + kk
                    for t in range(NT):
                        tok = slice(P * t, P * t + P)
                        last = product(ps[:, 4 + t, 0:CA], hT_hi[:, k, tok], hT_lo[:, k, tok], wh[:, kk, :], wl[:, kk, :],
                                       k == 0, k == KD - 1)
                        if k == KD - 1 and t < NT - 1:
                            last.then_inc(a_done, 1)
                used(last)

            def lru_gates(d, t0):
                pe.wait_ge(w_ready, t0 + tiles_in(t0))
                for part in range(2):
                    for n in range(NB):
                        if d == 0 and part == 0:
                            pe.wait_ge(xc_ready, n + 1)
                        if d == 0 and part == 1:
                            pe.wait_ge(pa_ready, n + 1)
                        if d == 1 and part == 0:
                            pe.wait_ge(v_ready, n + 1)
                        if d == 1 and part == 1:
                            pe.wait_ge(y_ready, n + 1)
                        col = slice(512 * part + P * n, 512 * part + P * n + P)
                        b = gate_bank(d, part, n)
                        last = product(ps[:, b, :], w_hi[:, t0 % 4, col], w_lo[:, t0 % 4, col],
                                       f_hi[:, FXC + n, :], f_lo[:, FXC + n, :], True, True)
                        if not (part and n == NB - 1):
                            last.then_inc(g_done, 1)
                used(last, tiles_in(t0))

            pe.wait_ge(xp_ready, NB)
            lru_gates(0, T_G0)
            for m in range(NB):
                pe.wait_ge(sig_ready, m + 1)
                used(cols_tile(T_Y + m, 0, m))
                if m == 1:
                    pe.wait_ge(pa_norm, NT)
                    for c in range(4):
                        pe.wait_ge(sig_ready, NB + c + 1)
                        lo, n = (P * c, P) if c < 3 else (CA - QK, QK)
                        for t in range(NT):
                            ins = nc.tensor.transpose(ps[0:n, 4 + c, P * t:P * t + P], pa[:, t, lo:lo + n], ident[:, :])
                        ins.then_inc(aT_done, 1)
            pe.wait_ge(aT_ready, 4)
            pe.wait_ge(w_ready, T_V + 1)
            for t in range(NT):
                tok = slice(P * t, P * t + P)
                last = product(ps[:, 4 + t, :], f_hi[:, FKVA, tok], f_lo[:, FKVA, tok],
                               w_hi[:, T_V % 4, 0:512], w_lo[:, T_V % 4, 0:512], True, True)
                if t < NT - 1:
                    last.then_inc(v_done, 1)
            used(last)
            lru_gates(1, T_G1)

            vs = f_hi[:, FV, :].rearrange("p (t c) -> p t c", t=NT)

            def q_and_k(h):
                dt = h * 4
                pe.wait_ge(w_ready, dt + T_HEAD + 1)
                for k in range(2):
                    col = slice(P * k, P * k + P)
                    last = product(ps[:, 0, :], w_hi[:, 0, col], w_lo[:, 0, col], f_hi[:, FQA + k, :], f_lo[:, FQA + k, :],
                                   k == 0, k == 1)
                used(last)
                pe.wait_ge(w_ready, dt + T_HEAD + 2)
                used(product(ps[:, 1, :], w_hi[:, 1, 0:P], w_lo[:, 1, 0:P], f_hi[:, FKVA, :], f_lo[:, FKVA, :], True, True))

            def weighted_values(h, kt):
                pe.wait_ge(pt_ready, h * 4 + kt + 1)

                def both():
                    return nc.tensor.matmul(ps[:, 4, :], vs[:, kt, :], f_hi[:, FPT + kt % 2, :], start=kt == 0, stop=kt == NT - 1)

                def small():
                    return nc.tensor.matmul(ps[0:VD, 4, :], vs[:, kt, 0:VD], f_lo[:, FPT + kt % 2, :], start=False, stop=False)

                if kt == 0:
                    both()
                    small().then_inc(pv_done, 1)
                else:
                    small()
                    both().then_inc(pv_done, 1)

            def wo_product(half, branch, j, c, ks):
                t0, m = T_R + 4 * half + 2 * branch + j, 4 * half + 2 * j + c
                wh, wl = split_view(w_hi, "wo", t0 % 4), split_view(w_lo, "wo", t0 % 4)
                if 0 in ks:
                    pe.wait_ge(w_ready, t0 + 1)
                if half:
                    pe.wait_ge(ra_gated if branch else rl_gated, m - 3)
                for k in ks:
                    if not half:
                        pe.wait_ge(ot_ready if branch else rec_ready, k + 1)
                    f = (FO if branch else FREC) + k
                    last = product(ps[:, 4 * branch + m % 4, :], wh[:, k, P * c:P * c + P],
                                   wl[:, k, P * c:P * c + P], f_hi[:, f, :], f_lo[:, f, :], k == 0, k == 3)
                if 3 in ks:
                    if c == 0:
                        last.then_inc(ra_done if branch else rl_done, 1)
                    else:
                        used(last)

            def head(h, more):
                dt = h * 4
                pe.wait_ge(gl_ready, h * 2 + 1)
                cols_tile(T_HEAD + 2, dt, 2, range(0, 5))
                pe.wait_ge(q_ready, h + 1)
                pe.wait_ge(k_ready, h + 1)
                pe.wait_ge(o_ready, h + 1)
                for t in range(NT):
                    tok = slice(P * t, P * t + P)
                    product(ps[:, 4 + t, :], f_hi[0:QK, FQ, tok], f_lo[0:QK, FQ, tok], f_hi[0:QK, FK, :], f_lo[0:QK, FK, :],
                            True, True).then_inc(sc_done, 1)
                used(cols_tile(T_HEAD + 2, dt, 2, range(5, KD)))
                pe.wait_ge(gl_ready, h * 2 + 2)
                cols_tile(T_HEAD + 3, dt, 3, range(0, 5))
                pe.wait_ge(p_ready, h * 4 + 4)
                for kt in range(NT):
                    for t in range(NT):
                        ins = nc.tensor.transpose(ps[:, 4 + kt, P * t:P * t + P], prob[:, t, P * kt:P * kt + P], ident[:, :])
                    ins.then_inc(t_done, 1)
                cols_tile(T_HEAD + 3, dt, 3, (5,))
                pe.wait_ge(vs_ready, h + 1)
                weighted_values(h, 0)
                used(cols_tile(T_HEAD + 3, dt, 3, (6, 7)))
                weighted_values(h, 1)
                if more:
                    q_and_k(h + 1)
                else:
                    wo_product(0, 0, 0, 0, range(0, 2))
                weighted_values(h, 2)
                weighted_values(h, 3)

            pe.wait_ge(sig_ready, 14)
            q_and_k(0)
            pe.wait_ge(sig_ready, 16)
            with pe.Fori(0, HEADS - 1) as h:
                head(h, True)
            head(HEADS - 1, False)

            wo_product(0, 0, 0, 0, (2,))
            wo_product(0, 0, 0, 1, range(0, 3))
            pe.wait_ge(gl_ready, 2 * HEADS + 2)
            for c in range(2):
                wo_product(0, 0, 1, c, range(0, 3))
            for j in range(2):
                for c in range(2):
                    wo_product(0, 0, j, c, (3,))
            pe.wait_ge(o_ready, HEADS + 1)
            for j in range(2):
                for c in range(2):
                    wo_product(0, 1, j, c, range(0, 4))
            for branch in range(2):
                for j in range(2):
                    for c in range(2):
                        wo_product(1, branch, j, c, range(0, 4))

            def w_out_product(n, kk, t):
                k, c, slot, wcol = 2 * (n % 4) + kk, n // 4, (T_OUT + n) % 4, slice(512 * kk, 512 * kk + 512)
                tok = slice(P * t, P * t + P)
                return product(ps[:, 4 * c + t, :], hT_hi[:, k, tok], hT_lo[:, k, tok],
                               w_hi[:, slot, wcol], w_lo[:, slot, wcol], k == 0, k == KD - 1)

            for n in range(4):
                pe.wait_ge(w_ready, T_OUT + n + 1)
                for kk in range(2):
                    k = 2 * n + kk
                    pe.wait_ge(mg_ready, k + 1)
                    if k == 0:
                        pe.wait_ge(rl_gated, KD)
                    for t in range(NT):
                        last = w_out_product(n, kk, t)
                        if k == KD - 1 and t < NT - 1:
                            last.then_inc(wo_done, 1)
                used(last)
            pe.wait_ge(ra_gated, KD)
            for t in range(NT):
                if t == NT - 1:
                    pe.wait_ge(x2_ready, NT)
                    transpose_half(xn, NT, 0, 0)
                for n in range(4, 8):
                    if t == 0:
                        pe.wait_ge(w_ready, T_OUT + n + 1)
                    for kk in range(2):
                        last = w_out_product(n, kk, t)
                    if t == NT - 1:
                        used(last)
                    elif n == 7:
                        last.then_inc(wo_done, 1)

            norm_and_tiles(xn, NT, 0, T_FFN, 4, h2_ready, bank_free=lambda j: pe.wait_ge(x2_ready, NT + j + 1))

            with pe.Fori(1, FT // 2) as i:
                for part in range(2):
                    for j in range(2):
                        pe.wait_ge(act_ready if part else silu_ready, i * 2 + j + 1)
                        used(cols_tile(T_FFN + 2 * part + j, i * 4, 4 + 2 * part + j))

            def down(n0, dn, toks):
                pe.wait_ge(w_ready, dn + T_DN + n0 + 1)
                pe.wait_ge(act_split, dn + n0 + 1)
                for t in toks:
                    for c in range(2):
                        last = down_part(n0, t, c, False)
                return last

            def down_part(n0, t, c, stop):
                a, s, tok = FACT + n0 % 4, n0 % 4, slice(P * t, P * t + P)
                return product(ps[:, 2 * t + c, :], f_hi[:, a, tok], f_lo[:, a, tok], w_hi[:, s, 512 * c:512 * c + 512],
                               w_lo[:, s, 512 * c:512 * c + 512], n0 == 0, stop)

            down(0, 0, (0, 1))
            pe.wait_ge(act_ready, FT + 2)
            pe.wait_ge(silu_ready, FT + 2)
            used(down(0, 0, (2, 3)))
            for n in (1, 2, 3):
                used(down(n, 0, range(NT)))
            with pe.Fori(0, 4) as i:
                for j in range(4):
                    used(down(4 + j, i * 4, range(NT)))
            pe.wait_ge(w_ready, T_DN + FT)
            pe.wait_ge(act_split, FT)
            for t in range(NT):
                for c in range(2):
                    down_part(FT - 2, t, c, False)
                    down_part(FT - 1, t, c, True).then_inc(dn_done, 1)


_INS = ["x", "norm1_g", "w_in", "q_a_norm_g", "w_q_b", "kv_a_norm_g", "w_kv_b", "w_o_attn", "conv_w", "conv_b",
        "w_rgate", "b_rgate", "w_igate", "b_igate", "lru_lambda", "w_o_lru", "w_out", "norm2_g", "w_ffn_gate",
        "w_ffn_up", "w_ffn_down", "final_g"]


def kernel(**inputs):
    import concourse.bacc as _bacc
    from concourse.bass_utils import run_bass_kernel_spmd as _run

    nc = _bacc.Bacc("TRN2", target_bir_lowering=False, num_devices=1, dynamic_dma_scratch_size=1024)
    arrays, args = {}, []
    tab_q, tab_k = rope_constants()
    for name, a in [(n, inputs[n]) for n in _INS] + [("rope_q", tab_q), ("rope_k", tab_k)]:
        a = np.ascontiguousarray(a)
        arrays[f"in_{name}_dram"] = a
        args.append(nc.dram_tensor(f"in_{name}_dram", a.shape, mybir.dt.from_np(a.dtype), kind="ExternalInput").ap())
    args.append(nc.dram_tensor("out_dram", (1, SEQ, D), F32, kind="ExternalOutput").ap())
    build(nc, *args)
    r = _run(nc, [arrays], core_ids=[0])
    return r.results[0]["out_dram"]
```
